# Optimizing a Trainium2 kernel written in Bass

```python
import jax, jax.numpy as jnp
from jax import lax
import numpy as np

D_MODEL = 2048
BATCH = 1
SEQ = 256
DEPTH = 1

N_MIXERS = 2
N_A_LAYERS = (DEPTH + N_MIXERS - 1) // N_MIXERS
N_B_LAYERS = DEPTH // N_MIXERS
HGRN_EXPAND = 128
HGRN_HEADS = D_MODEL // HGRN_EXPAND
HGRN_KEY_DIM = HGRN_HEADS * HGRN_EXPAND
HGRN_HEAD_V = D_MODEL // HGRN_HEADS
CHUNK = 64
CONV_WIDTH = 3
FFN_DIM = 5632
EPS = 1e-6


def rmsnorm(x, w):
    x32 = x.astype(jnp.float32)
    y = x32 * lax.rsqrt(jnp.mean(x32 * x32, axis=-1, keepdims=True) + EPS)
    return (y * w.astype(jnp.float32)).astype(x.dtype)

def dwconv3(z, w):
    L = z.shape[1]
    zp = jnp.pad(z, ((0, 0), (1, 1), (0, 0)))
    return w[0] * zp[:, :L] + w[1] * zp[:, 1:L + 1] + w[2] * zp[:, 2:]

def chunked_gated_recurrence(q, k, log_f, v):
    N, H, L, K = q.shape
    V = v.shape[-1]
    n_chunks = L // CHUNK

    def to_chunks(t):
        return t.reshape(N, H, n_chunks, CHUNK, t.shape[-1]).transpose(2, 0, 1, 3, 4)

    causal_in_chunk = jnp.tril(jnp.ones((CHUNK, CHUNK), dtype=bool))[:, :, None]

    def step(S, inp):
        qi, ki, gi, vi = inp
        b = jnp.cumsum(gi, axis=2)
        inter = jnp.einsum('nhtk,nhkv->nhtv', qi * jnp.exp(b), S)
        diff = b[:, :, :, None, :] - b[:, :, None, :, :]
        decay = jnp.exp(jnp.where(causal_in_chunk, diff, -jnp.inf))
        scores = jnp.einsum('nhtk,nhsk,nhtsk->nhts', qi, ki, decay)
        intra = jnp.einsum('nhts,nhsv->nhtv', scores, vi)
        b_last = b[:, :, -1]
        k_dec = ki * jnp.exp(b_last[:, :, None, :] - b)
        S_new = jnp.exp(b_last)[..., None] * S + jnp.einsum('nhck,nhcv->nhkv', k_dec, vi)
        return S_new, inter + intra

    S0 = jnp.zeros((N, H, K, V), jnp.float32)
    _, o = lax.scan(step, S0, (to_chunks(q), to_chunks(k), to_chunks(log_f), to_chunks(v)))
    return o.transpose(1, 2, 0, 3, 4).reshape(N, H, L, V)

def hgrn2_mixer(h, w_in, w_out, g_norm_w, lb_fwd, lb_bwd):
    B_, L, _ = h.shape
    K, D = HGRN_KEY_DIM, D_MODEL
    u = h @ w_in
    q, f_f, f_b, v, g = jnp.split(u, [K, 2 * K, 3 * K, 3 * K + D], axis=-1)
    q = jax.nn.silu(q)

    def gates(f_raw, lb):
        f = lb + (1.0 - lb) * jax.nn.sigmoid(f_raw.astype(jnp.float32))
        return 1.0 - f, jnp.log(f)

    k_f, lf_f = gates(f_f, lb_fwd)
    k_b, lf_b = gates(f_b, lb_bwd)

    def heads(t, d):
        return t.reshape(t.shape[0], L, HGRN_HEADS, d).transpose(0, 2, 1, 3).astype(jnp.float32)

    rev = lambda t: t[:, ::-1]
    qs = heads(jnp.concatenate([q, rev(q)], axis=0), HGRN_EXPAND)
    ks = heads(jnp.concatenate([k_f, rev(k_b)], axis=0), HGRN_EXPAND)
    ls = heads(jnp.concatenate([lf_f, rev(lf_b)], axis=0), HGRN_EXPAND)
    vs = heads(jnp.concatenate([v, rev(v)], axis=0), HGRN_HEAD_V)
    o = chunked_gated_recurrence(qs, ks, ls, vs)
    o = o[:B_] + o[B_:, :, ::-1]
    o = o.transpose(0, 2, 1, 3)
    gh = g.reshape(B_, L, HGRN_HEADS, HGRN_HEAD_V)
    o = rmsnorm(o, g_norm_w) * jax.nn.silu(gh.astype(jnp.float32))
    return o.reshape(B_, L, D).astype(h.dtype) @ w_out

def short_conv_mixer(h, w_in, w_conv, w_out):
    u = h @ w_in
    gate_b, gate_c, x_in = jnp.split(u, 3, axis=-1)
    z = dwconv3(gate_c * x_in, w_conv)
    return (gate_b * z) @ w_out

def conv_ffn(h, w_in, w_conv, w_out):
    up = dwconv3(h @ w_in, w_conv)
    gate, val = jnp.split(up, 2, axis=-1)
    return (jax.nn.silu(gate) * val) @ w_out

def first_inputs(seed: int = 0) -> dict:
    key = jax.random.key(seed)
    ks = jax.random.split(key, 16)
    D, K, F = D_MODEL, HGRN_KEY_DIM, FFN_DIM
    nrm = lambda k, shape, scale: jax.random.normal(k, shape, jnp.float32) * scale
    return {
        "x": nrm(ks[0], (BATCH, SEQ, D), 1.0),
        "hgrn_w_in": nrm(ks[1], (N_A_LAYERS, D, 3 * K + 2 * D), D ** -0.5),
        "hgrn_w_out": nrm(ks[2], (N_A_LAYERS, D, D), D ** -0.5),
        "hgrn_gnorm": 1.0 + nrm(ks[3], (N_A_LAYERS, HGRN_HEAD_V), 0.02),
        "hgrn_lower_bounds": nrm(ks[4], (2, N_A_LAYERS, K), 1.0),
        "sconv_w_in": nrm(ks[5], (N_B_LAYERS, D, 3 * D), D ** -0.5),
        "sconv_w_conv": nrm(ks[6], (N_B_LAYERS, CONV_WIDTH, D), CONV_WIDTH ** -0.5),
        "sconv_w_out": nrm(ks[7], (N_B_LAYERS, D, D), D ** -0.5),
        "ffn_w_in": nrm(ks[8], (DEPTH, D, 2 * F), D ** -0.5),
        "ffn_w_conv": nrm(ks[9], (DEPTH, CONV_WIDTH, 2 * F), CONV_WIDTH ** -0.5),
        "ffn_w_out": nrm(ks[10], (DEPTH, F, D), F ** -0.5),
        "norm_pre_mix": 1.0 + nrm(ks[11], (DEPTH, D), 0.02),
        "norm_post_mix": 1.0 + nrm(ks[12], (DEPTH, D), 0.02),
        "norm_pre_ffn": 1.0 + nrm(ks[13], (DEPTH, D), 0.02),
        "norm_post_ffn": 1.0 + nrm(ks[14], (DEPTH, D), 0.02),
    }

def first_block(x, hgrn_w_in, hgrn_w_out, hgrn_gnorm, hgrn_lower_bounds,
              sconv_w_in, sconv_w_conv, sconv_w_out,
              ffn_w_in, ffn_w_conv, ffn_w_out,
              norm_pre_mix, norm_post_mix, norm_pre_ffn, norm_post_ffn):
    lb = jnp.cumsum(jax.nn.softmax(hgrn_lower_bounds.astype(jnp.float32), axis=1), axis=1)
    lb = lb - lb[:, :1]
    for i in range(DEPTH):
        j = i // N_MIXERS
        h = rmsnorm(x, norm_pre_mix[i])
        if i % N_MIXERS == 0:
            m = hgrn2_mixer(h, hgrn_w_in[j], hgrn_w_out[j], hgrn_gnorm[j], lb[0, j], lb[1, j])
        else:
            m = short_conv_mixer(h, sconv_w_in[j], sconv_w_conv[j], sconv_w_out[j])
        x = x + rmsnorm(m, norm_post_mix[i])
        h = rmsnorm(x, norm_pre_ffn[i])
        x = x + rmsnorm(conv_ffn(h, ffn_w_in[i], ffn_w_conv[i], ffn_w_out[i]), norm_post_ffn[i])
    return x


HEAD_DIM = 128
SB_HEADS = D_MODEL // (2 * HEAD_DIM)
GDN_HEADS = D_MODEL // (2 * HEAD_DIM)
SB_WIDTH = SB_HEADS * HEAD_DIM
GDN_WIDTH = GDN_HEADS * HEAD_DIM
D_MIX = SB_WIDTH + GDN_WIDTH
N_IN = 3 * SB_WIDTH + 4 * GDN_WIDTH + 2 * GDN_HEADS
SB_BLOCK = 128
SHORT_CONV = 4
N_MEM = 256
X_HEADS = 4
X_HEAD_DIM = 128
X_WIDTH = X_HEADS * X_HEAD_DIM
D_FF = (11 * D_MODEL) // 4
FFN_CONV = 3


def rmsnorm_2(x, g):
    xf = x.astype(jnp.float32)
    y = xf * lax.rsqrt(jnp.mean(xf * xf, axis=-1, keepdims=True) + EPS)
    return (y * g.astype(jnp.float32)).astype(x.dtype)

def l2norm(x):
    return x * lax.rsqrt(jnp.sum(x * x, axis=-1, keepdims=True) + EPS)

def causal_dwconv(x, w):
    k = w.shape[0]
    return lax.conv_general_dilated(
        x, w[:, None, :].astype(x.dtype), window_strides=(1,), padding=[(k - 1, 0)],
        dimension_numbers=('NWC', 'WIO', 'NWC'), feature_group_count=x.shape[-1])

def stick_breaking_attention(q, k, v):
    b, s, h, dh = q.shape
    scale = dh ** -0.5
    n_blk = s // SB_BLOCK
    qb = jnp.moveaxis(q.reshape(b, n_blk, SB_BLOCK, h, dh), 1, 0)
    key_pos = jnp.arange(s)

    def block(args):
        q_blk, blk_idx = args
        z = jnp.einsum('bqhd,bshd->bhqs', q_blk, k) * scale
        q_pos = blk_idx * SB_BLOCK + jnp.arange(SB_BLOCK)
        valid = key_pos[None, :] < q_pos[:, None]
        log_beta = jax.nn.log_sigmoid(z)
        log_stay = jnp.where(valid, jax.nn.log_sigmoid(-z), 0.0)
        later = lax.cumsum(log_stay, axis=3, reverse=True) - log_stay
        weights = jnp.where(valid, jnp.exp(log_beta + later), 0.0)
        return jnp.einsum('bhqs,bshd->bqhd', weights, v)

    out = lax.map(block, (qb, jnp.arange(n_blk)))
    return jnp.moveaxis(out, 0, 1).reshape(b, s, h, dh)

def gated_delta_rule(q, k, v, beta, g):
    b, s, h, dk = q.shape
    dv = v.shape[-1]
    n = s // CHUNK

    def chunks(t):
        t = jnp.swapaxes(t, 1, 2)
        return t.reshape(b, h, n, CHUNK, *t.shape[3:])

    q, k, v, beta, g = chunks(q), chunks(k), chunks(v), chunks(beta), chunks(g)
    g_cum = jnp.cumsum(g, axis=-1)
    idx = jnp.arange(CHUNK)
    lower_incl = idx[:, None] >= idx[None, :]
    strict = idx[:, None] > idx[None, :]
    decay = jnp.exp(jnp.where(lower_incl, g_cum[..., :, None] - g_cum[..., None, :], -jnp.inf))
    k_beta = k * beta[..., None]
    v_beta = v * beta[..., None]
    lmat = jnp.where(strict, jnp.einsum('bhnid,bhnjd->bhnij', k_beta, k) * decay, 0.0)
    eye = jnp.eye(CHUNK, dtype=jnp.float32)
    t_inv = lax.linalg.triangular_solve(eye + lmat, jnp.broadcast_to(eye, lmat.shape),
                                        left_side=True, lower=True, unit_diagonal=True)
    u = t_inv @ v_beta
    w = t_inv @ (k_beta * jnp.exp(g_cum)[..., None])
    attn_intra = jnp.where(lower_incl, jnp.einsum('bhnid,bhnjd->bhnij', q, k) * decay, 0.0)
    q_decay = q * jnp.exp(g_cum)[..., None]
    k_tail = k * jnp.exp(g_cum[..., -1:] - g_cum)[..., None]
    chunk_decay = jnp.exp(g_cum[..., -1])

    def step(state, xs):
        u_c, w_c, qd_c, a_c, kt_c, cd_c = xs
        v_new = u_c - w_c @ state
        o = qd_c @ state + a_c @ v_new
        state = state * cd_c[..., None, None] + jnp.swapaxes(kt_c, -1, -2) @ v_new
        return state, o

    xs = tuple(jnp.moveaxis(t, 2, 0) for t in (u, w, q_decay, attn_intra, k_tail, chunk_decay))
    state0 = jnp.zeros((b, h, dk, dv), jnp.float32)
    _, o = lax.scan(step, state0, xs)
    o = jnp.moveaxis(o, 0, 2).reshape(b, h, s, dv)
    return jnp.swapaxes(o, 1, 2)

def gated_deltanet(q, k, v, z, b_logit, a_logit, conv_w, a_log, dt_bias, norm_g):
    bsz, s, _ = q.shape
    qkv = jnp.concatenate([q, k, v], axis=-1).astype(jnp.float32)
    qkv = jax.nn.silu(causal_dwconv(qkv, conv_w.astype(jnp.float32)))
    q, k, v = jnp.split(qkv, 3, axis=-1)
    heads = lambda t: t.reshape(bsz, s, GDN_HEADS, HEAD_DIM)
    q = l2norm(heads(q)) * (HEAD_DIM ** -0.5)
    k = l2norm(heads(k))
    v = heads(v)
    beta = jax.nn.sigmoid(b_logit.astype(jnp.float32))
    g = -jnp.exp(a_log.astype(jnp.float32)) * jax.nn.softplus(
        a_logit.astype(jnp.float32) + dt_bias.astype(jnp.float32))
    o = gated_delta_rule(q, k, v, beta, g)
    o = rmsnorm_2(o, norm_g) * jax.nn.silu(heads(z.astype(jnp.float32)))
    return o.reshape(bsz, s, GDN_WIDTH)

def memory_cross_attention(h, mem_n, w_q, w_kv, w_o):
    bsz, s, _ = h.shape
    m = mem_n.shape[1]
    q = (h @ w_q).reshape(bsz, s, X_HEADS, X_HEAD_DIM)
    k, v = jnp.split(mem_n @ w_kv, 2, axis=-1)
    k = k.reshape(bsz, m, X_HEADS, X_HEAD_DIM)
    v = v.reshape(bsz, m, X_HEADS, X_HEAD_DIM)
    logits = jnp.einsum('bshd,bmhd->bhsm', q.astype(jnp.float32), k.astype(jnp.float32)) * (X_HEAD_DIM ** -0.5)
    p = jax.nn.softmax(logits, axis=-1)
    o = jnp.einsum('bhsm,bmhd->bshd', p, v.astype(jnp.float32))
    return o.reshape(bsz, s, X_WIDTH).astype(h.dtype) @ w_o

def conv_ffn_2(h, w_up, conv_w, conv_b, w_down):
    u = causal_dwconv(h @ w_up, conv_w) + conv_b
    gate, up = jnp.split(u, 2, axis=-1)
    return (jax.nn.silu(gate) * up) @ w_down

def second_inputs(seed: int = 0) -> dict:
    key = jax.random.key(seed)
    ks = iter(jax.random.split(key, 32))
    f32 = jnp.float32
    nrm = lambda shape, scale: jax.random.normal(next(ks), shape, f32) * scale
    gain = lambda shape: 1.0 + 0.02 * jax.random.normal(next(ks), shape, f32)
    dt = jnp.exp(jax.random.uniform(next(ks), (DEPTH, GDN_HEADS), f32, np.log(1e-3), np.log(1e-1)))
    return {
        "x": jax.random.normal(next(ks), (BATCH, SEQ, D_MODEL), f32),
        "mem": jax.random.normal(next(ks), (BATCH, N_MEM, D_MODEL), f32),
        "mix_norm": gain((DEPTH, D_MODEL)),
        "w_in": nrm((DEPTH, D_MODEL, N_IN), D_MODEL ** -0.5),
        "gdn_conv": nrm((DEPTH, SHORT_CONV, 3 * GDN_WIDTH), SHORT_CONV ** -0.5),
        "gdn_a_log": jnp.log(jax.random.uniform(next(ks), (DEPTH, GDN_HEADS), f32, 1.0, 16.0)),
        "gdn_dt_bias": dt + jnp.log(-jnp.expm1(-dt)),
        "gdn_norm": gain((DEPTH, HEAD_DIM)),
        "w_out": nrm((DEPTH, D_MIX, D_MODEL), D_MIX ** -0.5),
        "xattn_norm": gain((DEPTH, D_MODEL)),
        "mem_norm": gain((DEPTH, D_MODEL)),
        "w_xq": nrm((DEPTH, D_MODEL, X_WIDTH), D_MODEL ** -0.5),
        "w_xkv": nrm((DEPTH, D_MODEL, 2 * X_WIDTH), D_MODEL ** -0.5),
        "w_xo": nrm((DEPTH, X_WIDTH, D_MODEL), X_WIDTH ** -0.5),
        "ffn_norm": gain((DEPTH, D_MODEL)),
        "w_up": nrm((DEPTH, D_MODEL, 2 * D_FF), D_MODEL ** -0.5),
        "ffn_conv": nrm((DEPTH, FFN_CONV, 2 * D_FF), FFN_CONV ** -0.5),
        "ffn_conv_bias": nrm((DEPTH, 2 * D_FF), 0.02),
        "w_down": nrm((DEPTH, D_FF, D_MODEL), D_FF ** -0.5),
        "final_norm": gain((D_MODEL,)),
    }

def second_block(x, mem, mix_norm, w_in, gdn_conv, gdn_a_log, gdn_dt_bias, gdn_norm, w_out,
              xattn_norm, mem_norm, w_xq, w_xkv, w_xo, ffn_norm, w_up, ffn_conv,
              ffn_conv_bias, w_down, final_norm):
    bsz, s, _ = x.shape
    cuts = [SB_WIDTH, 2 * SB_WIDTH, 3 * SB_WIDTH,
            3 * SB_WIDTH + GDN_WIDTH, 3 * SB_WIDTH + 2 * GDN_WIDTH,
            3 * SB_WIDTH + 3 * GDN_WIDTH, 3 * SB_WIDTH + 4 * GDN_WIDTH,
            3 * SB_WIDTH + 4 * GDN_WIDTH + GDN_HEADS]
    sb_heads = lambda t: t.astype(jnp.float32).reshape(bsz, s, SB_HEADS, HEAD_DIM)
    for l in range(DEPTH):
        h = rmsnorm_2(x, mix_norm[l])
        proj = h @ w_in[l]
        sq, sk, sv, gq, gk, gv, gz, gb, ga = jnp.split(proj, cuts, axis=-1)
        sb_out = stick_breaking_attention(sb_heads(sq), sb_heads(sk), sb_heads(sv))
        sb_out = sb_out.reshape(bsz, s, SB_WIDTH)
        gdn_out = gated_deltanet(gq, gk, gv, gz, gb, ga, gdn_conv[l], gdn_a_log[l],
                                 gdn_dt_bias[l], gdn_norm[l])
        mixed = jnp.concatenate([sb_out, gdn_out], axis=-1).astype(x.dtype)
        x = x + mixed @ w_out[l]
        mem_n = rmsnorm_2(mem, mem_norm[l])
        x = x + memory_cross_attention(rmsnorm_2(x, xattn_norm[l]), mem_n, w_xq[l], w_xkv[l], w_xo[l])
        x = x + conv_ffn_2(rmsnorm_2(x, ffn_norm[l]), w_up[l], ffn_conv[l], ffn_conv_bias[l], w_down[l])
    return rmsnorm_2(x, final_norm)


def setup_inputs(seed=0):
    out = dict(first_inputs(seed))
    for name, value in second_inputs(seed + 1).items():
        if name != "x":
            out[name + "_2"] = value
    return out


def reference(
    x, hgrn_w_in, hgrn_w_out, hgrn_gnorm, hgrn_lower_bounds, sconv_w_in, sconv_w_conv,
    sconv_w_out, ffn_w_in, ffn_w_conv, ffn_w_out, norm_pre_mix, norm_post_mix, norm_pre_ffn,
    norm_post_ffn, mem_2, mix_norm_2, w_in_2, gdn_conv_2, gdn_a_log_2, gdn_dt_bias_2,
    gdn_norm_2, w_out_2, xattn_norm_2, mem_norm_2, w_xq_2, w_xkv_2, w_xo_2, ffn_norm_2, w_up_2,
    ffn_conv_2, ffn_conv_bias_2, w_down_2, final_norm_2,
):
    x = first_block(
        x, hgrn_w_in, hgrn_w_out, hgrn_gnorm, hgrn_lower_bounds, sconv_w_in, sconv_w_conv,
        sconv_w_out, ffn_w_in, ffn_w_conv, ffn_w_out, norm_pre_mix, norm_post_mix, norm_pre_ffn,
        norm_post_ffn,
    )
    return second_block(
        x, mem_2, mix_norm_2, w_in_2, gdn_conv_2, gdn_a_log_2, gdn_dt_bias_2, gdn_norm_2,
        w_out_2, xattn_norm_2, mem_norm_2, w_xq_2, w_xkv_2, w_xo_2, ffn_norm_2, w_up_2,
        ffn_conv_2, ffn_conv_bias_2, w_down_2, final_norm_2,
    )


_drawn_inputs = setup_inputs


def setup_inputs(seed=0):
    import zlib

    import numpy as np

    out = dict(_drawn_inputs(seed))
    spreads = {}
    factors = {'hgrn_gnorm': 3.05,
     'norm_post_mix': 3.175,
     'norm_pre_ffn': 3.008,
     'norm_post_ffn': 4.327,
     'mix_norm_2': 5.502,
     'gdn_norm_2': 8.0,
     'xattn_norm_2': 8.0,
     'mem_norm_2': 8.0,
     'ffn_norm_2': 6.218,
     'ffn_conv_bias_2': 6.364,
     'final_norm_2': 2.807}
    for name, (base, spread) in spreads.items():
        noise = np.random.default_rng([zlib.crc32(name.encode()), seed]).standard_normal(out[name].shape)
        drawn = base * np.exp(spread * noise) if base else spread * noise
        out[name] = __import__('jax').numpy.asarray(drawn.astype(out[name].dtype))
    for name, factor in factors.items():
        out[name] = (out[name] * factor).astype(out[name].dtype)
    return out
```

```python
from contextlib import ExitStack

import numpy as np

import concourse.bass as bass
from concourse import mybir

F32 = mybir.dt.float32
F32R = mybir.dt.float32r
U8 = mybir.dt.uint8
ALU = mybir.AluOpType
ACT = mybir.ActivationFunctionType
AXX = mybir.AxisListType.X

P = 128
T = 256
D = 2048
DT = D // P
F = 5632
FT = F // P
EPS = 1e-6
HEADS = 16
SLOTS = 4
AHEAD = 3
BLK = 4 * 256
LEVELS = 7
F_MIN = 2.0 ** -63

VEC_PARTS = [("pre_mix", DT), ("post_mix", DT), ("pre_ffn", DT), ("post_ffn", DT), ("mix", DT),
             ("xattn", DT), ("mem", DT), ("ffn2", DT), ("final", DT), ("hgrn_gain", 1),
             ("gdn_gain", 1), ("bounds", 2 * HEADS), ("gdn_conv", 24 * 4), ("conv1", 2 * FT * 4),
             ("conv2", 2 * FT * 4)]
VEC_AT, VEC_N = {}, 0
for _name, _n in VEC_PARTS:
    VEC_AT[_name] = VEC_N
    VEC_N += _n

HG_GROUPS, HG_BLOCKS = 5 * 8, 4
UP_GROUPS = 2 * F // 256
DOWN_BLOCKS = F // 512
STREAM = [("hg", HG_GROUPS * 4), ("hgout", 8 * 4), ("up1", UP_GROUPS * 4), ("down1", 8 * DOWN_BLOCKS),
          ("mix", 28 * 4), ("mixout", 8 * 4), ("kv", 4 * 4), ("xq", 2 * 4), ("xo", 8 * 1),
          ("up2", UP_GROUPS * 4), ("down2", 8 * DOWN_BLOCKS)]
GROUPS = {"hg": 40, "hgout": 16, "up1": 44, "down1": 8, "mix": 28, "kv": 4, "mixout": 16, "xq": 2,
          "xo": 8, "up2": 44, "down2": 8}
BLOCK_AT, GROUP_AT, _b, _g = {}, {}, 0, 0
for _name, _n in STREAM:
    BLOCK_AT[_name], GROUP_AT[_name] = _b, _g
    _b += _n
    _g += GROUPS[_name]
N_BLOCKS = _b


class Steps:

    def __init__(self, sem, names):
        self.sem, self.names, self.n = sem, names, len(names)

    def count(self, name, turn=0):
        return self.n * turn + self.names.index(name) + 2

    def before(self, turn):
        return self.n * turn + 1


def drain(steps):
    for _ in steps:
        pass


def pause(n):
    for _ in range(n):
        yield


def slots(n, *sides):
    for _ in range(n):
        for s in sides:
            next(s, None)
        yield


def names(text):
    return text.split()


def build(nc, xT, memT, stream, tail, vecs, gates, consts, masks, outT):
    ctx = ExitStack()
    with ctx:
        def sb(name, shape, dt=F32, stack=None):
            return (stack or ctx).enter_context(nc.sbuf_tensor(name, shape, dt))

        def sem(name):
            return ctx.enter_context(nc.semaphore(name))

        raw = sb("raw", [P, SLOTS, BLK])
        whi = sb("whi", [P, SLOTS, BLK], F32R)
        wlo = sb("wlo", [P, SLOTS, BLK], F32R)
        half = sb("half", [P, 2, 2, T])
        x = sb("x", [P, DT, T])
        vec = sb("vec", [P, VEC_N])
        cst = sb("cst", [P, 4, P])
        msk = sb("msk", [P, LEVELS, P], U8)
        rr = sb("rr", [P, T])
        lnr = sb("lnr", [P, T])
        ident, ones, row_ge, row_le = (cst[:, c, :] for c in range(4))

        with ExitStack() as st:
            hs = sb("hs", [P, DT, 2 * T], F32R, st)
        with ExitStack() as st:
            m = sb("m", [P, DT, T], F32, st)
        hold = sb("hold", [P, DT, 2 * T])
        with ExitStack() as st:
            sq = sb("sq", [P, DT, T], F32, st)
        with ExitStack() as st:
            os_ = sb("os_", [P, DT, 2 * T], F32R, st)
            hin = sb("hin", [P, 2, 5, 2 * T], F32, st)
            sig = sb("sig", [P, 4, 2 * T], F32, st)
            qk = sb("qk", [P, 3, 2 * T], F32, st)
            lf = sb("lf", [P, 1 + 4 * T], F32, st)
            X = sb("X", [P, 4 * T + 2], F32, st)
            G = sb("G", [P, 2, 4 * T], F32, st)
            LU = sb("LU", [P, 2, 2, 2, P], F32, st)
            AD = sb("AD", [P, 4, P], F32, st)
            AO = sb("AO", [P, 2, 2, P], F32, st)
            vn = sb("vn", [P, 4, P], F32, st)
            tot = sb("tot", [P, 2, 8], F32, st)
            et = sb("et", [P, 2, 8], F32, st)
            reset = sb("reset", [P, 2 * T], F32, st)
            lb = sb("lb", [P, 2, HEADS], F32, st)
            oml = sb("oml", [P, 2, HEADS], F32, st)
        with ExitStack() as st:
            mixs = sb("mixs", [P, DT, 2 * T], F32R, st)
            gin = sb("gin", [P, 2, 4, 2, T + 3], F32, st)
            gts = sb("gts", [P, 2, 16], F32, st)
            gt2 = sb("gt2", [P, 6, 2, 8], F32, st)
            gaw = sb("gaw", [P, 16], F32, st)
            ea = sb("ea", [P, 8], F32, st)
            tl = sb("tl", [P, DT, 16], F32, st)
            tls = sb("tls", [P, 2, DT, 16], F32R, st)
            with ExitStack() as st2:
                sin = sb("sin", [P, 2, 3, 2 * T], F32, st2)
                neg = sb("neg", [P, 384], F32, st2)
                zm = sb("zm", [P, 2, 384], F32, st2)
                se = sb("se", [P, 2, 384], F32, st2)
                sp_ = sb("sp_", [P, 2, 384], F32, st2)
                svn = sb("svn", [P, 4, P], F32, st2)
            with ExitStack() as st2:
                gy = sb("gy", [P, 3, 2 * T], F32, st2)
                gs = sb("gs", [P, 4 * T], F32, st2)
                gr = sb("gr", [P, 4 * T], F32, st2)
                vb = sb("vb", [P, 4, P], F32, st2)
                kbe = sb("kbe", [P, 2, P], F32, st2)
                ktl = sb("ktl", [P, 2, P], F32, st2)
                gbm = sb("gbm", [P, 4, P], F32, st2)
                bbm = sb("bbm", [P, 4, P], F32, st2)
                DTr = sb("DTr", [P, 4, P], F32, st2)
                NLT = sb("NLT", [P, 4, P], F32, st2)
                ATr = sb("ATr", [P, 4, P], F32, st2)
                Tm = sb("Tm", [P, 4, P], F32, st2)
                TT = sb("TT", [P, 4, P], F32, st2)
                Y = sb("Y", [P, 4, P], F32, st2)
                u0 = sb("u0", [P, 2, P], F32, st2)
                Sm = sb("Sm", [P, 2, P], F32, st2)
                nwT = sb("nwT", [P, 2, P], F32, st2)
                vnw = sb("vnw", [P, 2, P], F32, st2)
                qd = sb("qd", [P, 2, P], F32, st2)
        with ExitStack() as st:
            sb("sq_again", [P, DT, T], F32, st)
            xs = sb("xs", [P, 4, 2 * T], F32R, st)
            mems = sb("mems", [P, DT, 2 * T], F32R, st)
            memr = sb("memr", [P, DT, T], F32, st)
            kv = sb("kv", [P, 8, T], F32, st)
            xq = sb("xq", [P, 4, T], F32, st)
        with ExitStack() as st:
            sb("sq_again2", [P, DT, T], F32, st)
            sb("xs_again", [P, 4, 2 * T], F32R, st)
            pr = sb("pr", [P, 8, T], F32, st)
            prT = sb("prT", [P, 4, 2, T], F32, st)
            xvn = sb("xvn", [P, 4, 2, P], F32, st)
            mx = sb("mx", [P, 8], F32, st)
            sm = sb("sm", [P, 8], F32, st)
            rs = sb("rs", [P, 8], F32, st)
        with ExitStack() as st:
            acts = sb("acts", [P, FT, 2 * T], F32R, st)
            cin = sb("cin", [P, 4, T + 2], F32, st)
            cy = sb("cy", [P, 4, T], F32, st)

        acc = ctx.enter_context(nc.psum_tensor("acc", [P, 4, 512], F32))
        ps = ctx.enter_context(nc.psum_tensor("ps", [P, 4, 512], F32))

        raw_in = [sem(f"raw_in{b}") for b in range(SLOTS)]
        hi_ready = sem("hi_ready")
        lo_ready = sem("lo_ready")
        blk_used = sem("blk_used")
        half_out = sem("half_out")
        evac = sem("evac")
        const_in, mem_in, out_done = sem("const_in"), sem("mem_in"), sem("out_done")

        nrm_names = []
        for s, kind in (("n1", "pre"), ("n2", "post"), ("n3", "pre"), ("n4", "post"), ("n5", "pre"),
                        ("n6", "add"), ("n7", "pre"), ("n8", "pre"), ("n9", "add"), ("n10", "pre"),
                        ("n11", "add"), ("n12", "final")):
            nrm_names.append((s, kind))
        nA, nV, nP = [], [], []
        for s, kind in nrm_names:
            if kind != "add":
                nA += [f"{s}_sq{c}" for c in range(4)] + [f"{s}_ln", f"{s}_r"]
                nP += [f"{s}_ssq"]
            if kind == "pre":
                nA += [f"{s}_hi{c}" for c in range(4)]
                nV += [f"{s}_{w}{c}" for c in range(4) for w in ("h", "lo")]
            elif kind == "post":
                nV += [f"{s}_{w}{c}" for c in range(4) for w in ("t", "x")]
            else:
                nV += [f"{s}_{'x' if kind == 'add' else 'h'}{c}" for c in range(4)]
        norm_act = Steps(sem("norm_act"), nA)
        norm_vec = Steps(sem("norm_vec"), nV)
        norm_pe = Steps(sem("norm_pe"), nP)
        hg_act = Steps(sem("hg_act"), names("ex et er vn e1 ad ao e2 e3 e4 e5 e6"))
        hg_act_in = Steps(sem("hg_act_in"), names("sig ln"))
        hg_vec_in = Steps(sem("hg_vec_in"), names("g f clamp"))
        hg_act_out = Steps(sem("hg_act_out"), names("osq oln or"))
        hg_vec = Steps(sem("hg_vec"), names(
            "q k bf bb totf totb er g64l g64u lu1 lu0 ks d1l d1u p1l p1u c0 "
            "d2l d2u p2l p2u c1 d3l d3u p3l p3u c2 d4l d4u p4l p4u c3 "
            "d5l d5u p5l p5u c4 d6l d6u p6l p6u c5 c6"))
        hg_vec_out = Steps(sem("hg_vec_out"), names("og os hi lo"))
        hg_pe = Steps(sem("hg_pe"), names("vt diag l128 g0 g1 g2 g3 g4 g5 g6"))
        hg_pe_out = Steps(sem("hg_pe_out"), names("pv ssq"))
        part_sum = sem("part_sum")
        copies_begun = sem("copies_begun")
        gate_in, neg_in, gpad_set, mem_out = sem("gate_in"), sem("neg_in"), sem("gpad_set"), sem("mem_out")
        gt_act = Steps(sem("gt_act"), names("tlh ea beta abs e l egc egt"))
        gt_vec = Steps(sem("gt_vec"), names("tll a sp g cum tot bgc"))
        gt_pe = Steps(sem("gt_pe"), names("lg cum"))
        sb_act = Steps(sem("sb_act"), names("vn abs e l w hi"))
        sb_vec = Steps(sem("sb_vec"), names("zm sp w lo"))
        sb_pe = Steps(sem("sb_pe"), names("z cs o"))
        gd_act = Steps(sem("gd_act"), names(
            "silu sqk ln r qe dt vb kbe ktl y0 y1 y2 y3 y4 y5 y6 u0 nw"))
        gd_act_out = Steps(sem("gd_act_out"), names("vn osq oln or"))
        gd_vec = Steps(sem("gd_vec"), names(
            "c0 c1 c2 c3 gbm bbm q k d nl0 at0 nl at qd Tm TT "
            "t0 tt0 t1 tt1 t2 tt2 t3 tt3 t4 tt4 t5 tt5 t6 tt6 S"))
        gd_vec_out = Steps(sem("gd_vec_out"), names("og os hi lo"))
        gd_pe = Steps(sem("gd_pe"), names(
            "ssq rows kk tr y0 z0 y1 z1 y2 z2 y3 z3 y4 z4 y5 z5 y6 z6 uw S"))
        gd_pe_out = Steps(sem("gd_pe_out"), names("vn o os"))
        xa_act = Steps(sem("xa_act"), names("p vn pt hi"))
        xa_vec = Steps(sem("xa_vec"), names("mx nmx rs p lo"))
        xa_pe = Steps(sem("xa_pe"), names("z vt pt o"))
        hg_exp = sem("hg_exp")
        hg_set = sem("hg_set")
        mlp_vec = [Steps(sem(f"mlp_vec{k}"), names(
            "a00 a01 a10 a11 a20 a21 b00 b01 b10 b11 b20 b21 mul hi lo")) for k in range(2)]
        mlp_act = [Steps(sem(f"mlp_act{k}"), names("silu")) for k in range(2)]
        pad_set = [sem(f"pad_set{k}") for k in range(2)]

        def at(lap, k):
            return lap + k // SLOTS, k % SLOTS

        def round_hi(act, lap, k):
            r, b = at(lap, k)
            act.wait_ge(raw_in[b], 16 * r + 16)
            act.wait_ge(blk_used, SLOTS * r + b + 1)
            nc.scalar.activation(whi[:, b, :], raw[:, b, :], ACT.Copy).then_inc(hi_ready, 1)

        def take_lo(dve, lap, k):
            r, b = at(lap, k)
            dve.wait_ge(hi_ready, SLOTS * r + b + 1)
            nc.vector.tensor_tensor(wlo[:, b, :], raw[:, b, :], whi[:, b, :].bitcast(F32),
                                    ALU.subtract).then_inc(lo_ready, 1)

        def copy_half(act, lap, k, group, par):
            r, b = at(lap, k)
            act.wait_ge(blk_used, SLOTS * r + b + 1 + SLOTS)
            act.wait_ge(evac, group + 1)
            nc.scalar.activation(half[:, par], acc[:, 2 * par:2 * par + 2, T:2 * T],
                                 ACT.Copy).then_inc(half_out, 1)

        def evacuate(dve, dest, group, par):
            dve.wait_ge(half_out, group + 1)
            nc.vector.tensor_tensor(dest, acc[:, 2 * par:2 * par + 2, 0:T], half[:, par],
                                    ALU.add).then_inc(evac, 1)

        def multiply(pe, lap, k, group, par, src, kb, first, last, side=None):
            r, b = at(lap, k)
            if kb == first:
                pe.wait_ge(evac, group + 1)
            pe.wait_ge(lo_ready, SLOTS * r + b + 1 + SLOTS)
            for n in range(2):
                for q in range(4):
                    c, kt = q * 256 + n * P, 4 * kb + q
                    nc.tensor.matmul(acc[:, 2 * par + n, :], whi[:, b, c:c + P], src[:, kt, :],
                                     start=(kt == 4 * first), stop=False)
                    mm = nc.tensor.matmul(acc[:, 2 * par + n, 0:T], wlo[:, b, c:c + P],
                                          src[:, kt, 0:T], start=False, stop=(kt == 4 * last + 3))
                if n == 1:
                    mm.then_inc(blk_used, 1)
                if side is not None:
                    next(side, None)

        def norm_scalar(act, s, kind, src, ready, dst=hs):
            for c in range(4):
                ready(act, c)
                nc.scalar.activation(sq[:, 4 * c:4 * c + 4, :],
                                                   src[:, 4 * c:4 * c + 4, :], ACT.Square).then_inc(norm_act.sem, 1)
            act.wait_ge(norm_pe.sem, norm_pe.count(f"{s}_ssq"))
            nc.scalar.activation(lnr[:], ps[:, 0, 0:T], ACT.Ln, bias=EPS,
                                               scale=1.0 / D).then_inc(norm_act.sem, 1)
            act.wait_ge(norm_act.sem, norm_act.count(f"{s}_ln"))
            nc.scalar.activation(rr[:], lnr[:], ACT.Exp, scale=-0.5).then_inc(norm_act.sem, 1)
            if kind == "pre":
                for c in range(4):
                    act.wait_ge(norm_vec.sem, norm_vec.count(f"{s}_h{c}"))
                    nc.scalar.activation(dst[:, 4 * c:4 * c + 4, 0:T],
                                                       sq[:, 4 * c:4 * c + 4, :], ACT.Copy).then_inc(norm_act.sem, 1)

        def norm_tensor(pe, s):
            for t in range(DT):
                if t % 4 == 0:
                    pe.wait_ge(norm_act.sem, norm_act.count(f"{s}_sq{t // 4}"))
                mm = nc.tensor.matmul(ps[:, 0, 0:T], ones, sq[:, t, :], start=(t == 0), stop=(t == DT - 1))
            mm.then_inc(norm_pe.sem, 1)

        def norm_pre_vector(dve, s, gain, dst, src=x):
            dve.wait_ge(norm_act.sem, norm_act.count(f"{s}_r"))
            for c in range(4):
                for t in range(4 * c, 4 * c + 4):
                    g = VEC_AT[gain] + t
                    ins = nc.vector.scalar_tensor_tensor(sq[:, t, :], src[:, t, :], vec[:, g:g + 1],
                                                         rr[:], ALU.mult, ALU.mult)
                ins.then_inc(norm_vec.sem, 1)
                if dst is None:
                    continue
                dve.wait_ge(norm_act.sem, norm_act.count(f"{s}_hi{c}"))
                nc.vector.tensor_tensor(
                    dst[:, 4 * c:4 * c + 4, T:2 * T], sq[:, 4 * c:4 * c + 4, :],
                    dst[:, 4 * c:4 * c + 4, 0:T].bitcast(F32), ALU.subtract).then_inc(norm_vec.sem, 1)

        def norm_post_vector(dve, s, gain):
            dve.wait_ge(norm_act.sem, norm_act.count(f"{s}_r"))
            for c in range(4):
                for t in range(4 * c, 4 * c + 4):
                    g = VEC_AT[gain] + t
                    ins = nc.vector.scalar_tensor_tensor(m[:, t, :], m[:, t, :], vec[:, g:g + 1],
                                                         rr[:], ALU.mult, ALU.mult)
                ins.then_inc(norm_vec.sem, 1)
                dve.wait_ge(norm_vec.sem, norm_vec.count(f"{s}_t{c}"))
                nc.vector.tensor_tensor(x[:, 4 * c:4 * c + 4, :], x[:, 4 * c:4 * c + 4, :],
                                                      m[:, 4 * c:4 * c + 4, :], ALU.add).then_inc(norm_vec.sem, 1)

        def add_vector(dve, s, name, first=0):
            for c in range(4):
                dve.wait_ge(evac, GROUP_AT[name] + first + 2 * c + 1 + 3)
                nc.vector.tensor_tensor(x[:, 4 * c:4 * c + 4, :], x[:, 4 * c:4 * c + 4, :],
                                                      m[:, 4 * c:4 * c + 4, :], ALU.add).then_inc(norm_vec.sem, 1)

        def product(eng, what, name, kbs, loops, per_loop, src=None, last=False, dest=m):
            lap0, g0 = BLOCK_AT[name] // SLOTS, GROUP_AT[name]
            laps = per_loop * kbs // SLOTS

            def body(i, final):
                lap, g = lap0 + laps * i, g0 + per_loop * i
                for k in range(per_loop * kbs):
                    grp, kb = divmod(k, kbs)
                    ahead = not (final and k + AHEAD >= per_loop * kbs)
                    if what == "act":
                        if ahead:
                            round_hi(eng, lap, k + AHEAD)
                        if kb == kbs - 1:
                            copy_half(eng, lap, k, g + grp, grp % 2)
                    elif what == "dve":
                        if ahead:
                            take_lo(eng, lap, k + AHEAD)
                        if kb == kbs - 1:
                            evacuate(eng, dest[:, bass.ds((per_loop * i + grp) * 2, 2), :], g + grp, grp % 2)
                    else:
                        multiply(eng, lap, k, g + grp, grp % 2, src, kb, 0, kbs - 1)

            if last or loops == 1:
                for i in range(loops):
                    body(i, last and i == loops - 1)
            else:
                with eng.Fori(0, loops) as i:
                    body(i, False)

        def split_product(eng, what, name, src, sums, side):
            lap, g = BLOCK_AT[name] // SLOTS, GROUP_AT[name]
            for k in range(24):
                grp, kb = divmod(k, 3)
                if what == "act":
                    round_hi(eng, lap, k + AHEAD)
                    next(side, None)
                    if kb == 2:
                        copy_half(eng, lap, k, g + grp, grp % 2)
                elif what == "dve":
                    take_lo(eng, lap, k + AHEAD)
                    next(side, None)
                    if kb == 2:
                        evacuate(eng, m[:, 2 * grp:2 * grp + 2, :], g + grp, grp % 2)
                else:
                    multiply(eng, lap, k, g + grp, grp % 2, src, kb, 0, 2, side)
            drain(side)
            if what == "pe":
                if name == "hgout":
                    eng.wait_ge(hg_vec_out.sem, hg_vec_out.count("lo", 7))
                else:
                    eng.wait_ge(gd_vec_out.sem, gd_vec_out.count("lo", 3))
            for grp in range(8):
                k, ga, par = 24 + grp, g + 8 + grp, grp % 2
                if what == "act":
                    round_hi(eng, lap, k + AHEAD)
                    copy_half(eng, lap, k, ga, par)
                elif what == "dve":
                    take_lo(eng, lap, k + AHEAD)
                    eng.wait_ge(half_out, ga + 1)
                    nc.vector.tensor_tensor(half[:, par], acc[:, 2 * par:2 * par + 2, 0:T], half[:, par],
                                            ALU.add).then_inc(part_sum, 1)
                    eng.wait_ge(part_sum, sums + grp + 1)
                    eng.wait_ge(evac, g + grp + 3)
                    mt = m[:, 2 * grp:2 * grp + 2, :]
                    nc.vector.tensor_tensor(mt, mt, half[:, par], ALU.add).then_inc(evac, 1)
                else:
                    multiply(eng, lap, k, ga, par, src, 3, 3, 3)

        def halves(ap, h):
            return ap.rearrange("p d (n u h) -> p d n u h", u=2, h=h)

        def Xd():
            return X[:, 0:4 * T].rearrange("p (d n) -> p d n", d=2)

        def middle(h):
            v = X[:, :].rearrange("p (d n) -> p d n", d=2)
            return v[:, :, h - 1:2 * T:2 * h].unsqueeze(3).broadcast_to([P, 2, T // h, h])

        EXv = sig[:, 0:2, :]
        ERv = sig[:, 2:4, :]
        LOWER, UPPER = qk[:, 0:2, :], qk[:, 1:3, :]

        def hg_vector_in(dve, turn, par):
            n = hin[:, par]
            yield from pause(18)
            dve.wait_ge(hg_act_in.sem, hg_act_in.count("sig", turn))
            nc.vector.tensor_tensor(n[:, 3], n[:, 3], sig[:, 3], ALU.mult).then_inc(hg_vec_in.sem, 1)
            for d in range(2):
                for h in range(2):
                    ins = nc.vector.tensor_scalar(
                        sig[:, d, h * T:(h + 1) * T], sig[:, d, h * T:(h + 1) * T],
                        oml[:, d, bass.ds(2 * turn + h, 1)], lb[:, d, bass.ds(2 * turn + h, 1)],
                        ALU.mult, ALU.add)
            ins.then_inc(hg_vec_in.sem, 1)
            dve.wait_ge(hg_vec_in.sem, hg_vec_in.count("f", turn))
            nc.vector.tensor_scalar(
                lf[:, 1:1 + 4 * T], sig[:, 0:2, :].rearrange("p d n -> p (d n)"), F_MIN, None,
                ALU.max).then_inc(hg_vec_in.sem, 1)

        def hg_vector(dve, turn, par):
            n = hin[:, par]
            dve.wait_ge(hg_pe.sem, hg_pe.before(turn))
            nc.vector.tensor_tensor(qk[:, 1], n[:, 2], sig[:, 2], ALU.mult).then_inc(hg_vec.sem, 1)
            nc.vector.tensor_scalar(qk[:, 0:3:2, :], sig[:, 0:2, :], -1.0, 1.0, ALU.mult,
                                                ALU.add).then_inc(hg_vec.sem, 1)
            dve.wait_ge(hg_act_in.sem, hg_act_in.count("ln", turn))
            nc.vector.tensor_tensor_scan(X[:, 0:2 * T], reset[:], lf[:, 1:1 + 2 * T], 0.0,
                                                     ALU.mult, ALU.add).then_inc(hg_vec.sem, 1)
            nc.vector.tensor_tensor_scan(X[:, 2 * T:4 * T], lf[:, 2 * T:4 * T], reset[:], 0.0,
                                                     ALU.add, ALU.mult).then_inc(hg_vec.sem, 1)
            yield
            dve.wait_ge(hg_vec.sem, hg_vec.count("bb", turn))
            last = X[:, 0:4 * T].rearrange("p (d c n) -> p d c n", d=2, n=64)[:, :, :, 63]
            lastf = lf[:, 1:1 + 4 * T].rearrange("p (d c n) -> p d c n", d=2, n=64)[:, 1, :, 63]
            nc.vector.tensor_copy(tot[:, 0, :], last[:, 0, :]).then_inc(hg_vec.sem, 1)
            nc.vector.tensor_tensor(tot[:, 1, :], last[:, 1, :], lastf, ALU.add).then_inc(hg_vec.sem, 1)
            dve.wait_ge(hg_vec.sem, hg_vec.count("totb", turn))
            nc.vector.tensor_tensor(
                G[:, 0].rearrange("p (c n) -> p c n", n=64),
                tot[:].rearrange("p d c -> p (d c)").unsqueeze(2).broadcast_to([P, 16, 64]),
                X[:, 0:4 * T].rearrange("p (c n) -> p c n", n=64), ALU.subtract).then_inc(hg_vec.sem, 1)
            yield from pause(3)
            dve.wait_ge(hg_act.sem, hg_act.count("er", turn))
            g = halves(G[:, 0].rearrange("p (d n) -> p d n", d=2), 64)
            lo_, up_ = halves(LOWER, 64), halves(UPPER, 64)
            ex_, er_ = halves(EXv, 64), halves(ERv, 64)
            nc.vector.tensor_tensor(g[:, :, :, 0, :], lo_[:, :, :, 0, :], er_[:, :, :, 0, :],
                                                ALU.mult).then_inc(hg_vec.sem, 1)
            nc.vector.tensor_tensor(g[:, :, :, 1, :], up_[:, :, :, 1, :], ex_[:, :, :, 1, :],
                                                ALU.mult).then_inc(hg_vec.sem, 1)
            yield

            def chunk(ap, c):
                return ap.rearrange("p d (h c n) -> p d h c n", h=2, n=64)[:, :, :, c, :]

            def whole(c):
                return et[:, :, c:8:4].unsqueeze(3).broadcast_to([P, 2, 2, 64])

            nc.vector.tensor_tensor(LU[:, 0, :, :, 64:128], chunk(LOWER, 1), chunk(ERv, 1), ALU.mult)
            nc.vector.tensor_tensor(LU[:, 1, :, :, 0:64], chunk(UPPER, 2), chunk(EXv, 2),
                                                ALU.mult).then_inc(hg_vec.sem, 1)
            dve.wait_ge(hg_vec.sem, hg_vec.count("g64u", turn))
            G0 = G[:, 0].rearrange("p (d n) -> p d n", d=2)
            nc.vector.tensor_tensor(LU[:, 0, :, :, 0:64], chunk(G0, 0), whole(1), ALU.mult)
            nc.vector.tensor_tensor(LU[:, 1, :, :, 64:128], chunk(G0, 3), whole(2),
                                                ALU.mult).then_inc(hg_vec.sem, 1)
            nc.vector.tensor_tensor(n[:, 2], qk[:, 0], qk[:, 2], ALU.add).then_inc(hg_vec.sem, 1)
            yield
            for lv in range(1, LEVELS):
                h = 64 >> lv
                s = lv % 2
                gl = G[:, s].rearrange("p (d n) -> p d n", d=2)
                if lv >= 2:
                    dve.wait_ge(hg_pe.sem, hg_pe.count(f"g{lv - 2}", turn))
                nc_low, nc_up = halves(gl, h)[:, :, :, 0, :], halves(gl, h)[:, :, :, 1, :]
                nc.vector.tensor_tensor(nc_low, middle(h), halves(Xd(), h)[:, :, :, 0, :],
                                                    ALU.subtract).then_inc(hg_vec.sem, 1)
                nc.vector.tensor_tensor(nc_up, halves(Xd(), h)[:, :, :, 1, :], middle(h),
                                                    ALU.subtract).then_inc(hg_vec.sem, 1)
                yield
                dve.wait_ge(hg_act.sem, hg_act.count(f"e{lv}", turn))
                nc.vector.tensor_tensor(nc_low, nc_low, halves(LOWER, h)[:, :, :, 0, :],
                                                    ALU.mult).then_inc(hg_vec.sem, 1)
                nc.vector.tensor_tensor(nc_up, nc_up, halves(UPPER, h)[:, :, :, 1, :],
                                                    ALU.mult).then_inc(hg_vec.sem, 1)
                merge(dve, turn, lv - 1)
                yield
            yield
            merge(dve, turn, LEVELS - 1)

        out_sq, out_rms = G[:, 1, 0:2 * T], G[:, 1, 2 * T:4 * T]

        def hg_vector_out(dve, turn, par):
            n = hin[:, par]
            yield from pause(3)
            dve.wait_ge(hg_act_out.sem, hg_act_out.count("or", turn))
            og = out_sq
            gain = vec[:, VEC_AT["hgrn_gain"]:VEC_AT["hgrn_gain"] + 1]
            nc.vector.scalar_tensor_tensor(og, ps[:, 0, :], gain, out_rms, ALU.mult, ALU.mult).then_inc(hg_vec_out.sem, 1)
            dve.wait_ge(hg_vec_out.sem, hg_vec_out.count("og", turn))
            nc.vector.tensor_tensor(og, og, n[:, 3], ALU.mult).then_inc(hg_vec_out.sem, 1)
            dve.wait_ge(hg_vec_out.sem, hg_vec_out.count("os", turn))
            o2 = og.rearrange("p (h t) -> p h t", h=2)
            dst = os_[:, bass.ds(2 * turn, 2), :]
            nc.vector.tensor_scalar(dst[:, :, 0:T], o2, 1.0, None, ALU.mult).then_inc(hg_vec_out.sem, 1)
            dve.wait_ge(hg_vec_out.sem, hg_vec_out.count("hi", turn))
            nc.vector.tensor_tensor(dst[:, :, T:2 * T], o2, dst[:, :, 0:T].bitcast(F32),
                                                ALU.subtract).then_inc(hg_vec_out.sem, 1)

        def merge(dve, turn, lv):
            dve.wait_ge(hg_pe.sem, hg_pe.count(f"g{lv}", turn))
            if lv == 0:
                dve.wait_ge(hg_act.sem, hg_act.count("ad", turn))
            else:
                dve.wait_ge(hg_vec.sem, hg_vec.count(f"c{lv - 1}", turn))
            dve.sem_inc(copies_begun, 1)
            nc.vector.copy_predicated(
                AD[:], msk[:, lv, :].unsqueeze(1).broadcast_to([P, 4, P]),
                ps[:, 2 + lv % 2, :].rearrange("p (a b) -> p a b", a=4)).then_inc(hg_vec.sem, 1)

        def hg_scalar_in(act, turn, par):
            yield from pause(16)
            act.wait_ge(evac, GROUP_AT["hg"] + 5 * turn + 3 + 3)
            nc.scalar.activation(sig[:], hin[:, par, 0:4], ACT.Sigmoid).then_inc(hg_act_in.sem, 1)
            yield from pause(3)
            act.wait_ge(hg_vec_in.sem, hg_vec_in.count("clamp", turn))
            nc.scalar.activation(lf[:, 1:1 + 4 * T], lf[:, 1:1 + 4 * T], ACT.Ln).then_inc(hg_act_in.sem, 1)

        def hg_scalar(act, turn, par):
            yield
            act.wait_ge(hg_vec.sem, hg_vec.count("bb", turn))
            nc.scalar.activation(EXv, Xd(), ACT.Exp).then_inc(hg_act.sem, 1)
            yield
            act.wait_ge(hg_vec.sem, hg_vec.count("er", turn))
            nc.scalar.activation(et[:], tot[:], ACT.Exp).then_inc(hg_act.sem, 1)
            nc.scalar.activation(ERv, G[:, 0].rearrange("p (d n) -> p d n", d=2), ACT.Exp).then_inc(hg_act.sem, 1)
            yield
            act.wait_ge(hg_pe.sem, hg_pe.count("vt", turn))
            nc.scalar.activation(vn[:].rearrange("p a b -> p (a b)"), ps[:, 1, :], ACT.Copy).then_inc(hg_act.sem, 1)
            yield from pause(4)
            act.wait_ge(hg_vec.sem, hg_vec.count("d1u", turn))
            nc.scalar.activation(G[:, 1], G[:, 1], ACT.Exp).then_inc(hg_act.sem, 1)
            act.wait_ge(hg_pe.sem, hg_pe.count("diag", turn))
            nc.scalar.activation(AD[:].rearrange("p a b -> p (a b)"), ps[:, 1, :], ACT.Copy).then_inc(hg_act.sem, 1)
            act.wait_ge(hg_pe.sem, hg_pe.count("l128", turn))
            nc.scalar.activation(AO[:].rearrange("p d h b -> p (d h b)"), ps[:, 0, :], ACT.Copy).then_inc(hg_act.sem, 1)
            for lv in range(2, LEVELS):
                yield from pause(2)
                act.wait_ge(hg_vec.sem, hg_vec.count(f"d{lv}u", turn))
                nc.scalar.activation(G[:, lv % 2], G[:, lv % 2], ACT.Exp).then_inc(hg_act.sem, 1)

        def hg_scalar_out(act, turn, par):
            yield
            act.wait_ge(hg_pe_out.sem, hg_pe_out.count("pv", turn))
            nc.scalar.activation(out_sq, ps[:, 0, :], ACT.Square).then_inc(hg_act_out.sem, 1)
            yield
            act.wait_ge(hg_pe_out.sem, hg_pe_out.count("ssq", turn))
            nc.scalar.activation(out_rms, ps[:, 2, :], ACT.Ln, bias=EPS, scale=1.0 / P).then_inc(hg_act_out.sem, 1)
            act.wait_ge(hg_act_out.sem, hg_act_out.count("oln", turn))
            nc.scalar.activation(out_rms, out_rms, ACT.Exp, scale=-0.5).then_inc(hg_act_out.sem, 1)

        def hg_tensor(pe, turn, par):
            n = hin[:, par]
            yield from pause(3)
            pe.wait_ge(hg_vec.sem, hg_vec.before(turn))
            pe.wait_ge(evac, GROUP_AT["hg"] + 5 * turn + 4 + 3)
            for a in range(4):
                mm = nc.tensor.transpose(ps[:, 1, a * P:(a + 1) * P], n[:, 4, a * P:(a + 1) * P], ident)
            mm.then_inc(hg_pe.sem, 1)
            yield from pause(10)
            pe.wait_ge(hg_act.sem, hg_act.count("vn", turn))
            pe.wait_ge(hg_vec.sem, hg_vec.count("ks", turn))
            for a in range(4):
                mm = nc.tensor.matmul(ps[:, 1, a * P:(a + 1) * P], n[:, 2, a * P:(a + 1) * P],
                                      qk[:, 1, a * P:(a + 1) * P], start=True, stop=True)
            mm.then_inc(hg_pe.sem, 1)
            for d in range(2):
                for h in range(2):
                    mm = nc.tensor.matmul(ps[:, 0, (2 * d + h) * P:(2 * d + h + 1) * P], LU[:, d, d, h, :],
                                          LU[:, 1 - d, d, h, :], start=True, stop=True)
            mm.then_inc(hg_pe.sem, 1)
            yield
            for lv in range(LEVELS):
                if lv == 0:
                    pe.wait_ge(hg_vec.sem, hg_vec.count("ks", turn))
                else:
                    pe.wait_ge(hg_vec.sem, hg_vec.count(f"p{lv}u", turn))
                if lv >= 2:
                    pe.wait_ge(hg_vec.sem, hg_vec.count(f"c{lv - 2}", turn))
                for d in range(2):
                    for a in range(4):
                        g = G[:, lv % 2, (4 * d + a) * P:(4 * d + a + 1) * P]
                        o = ps[:, 2 + lv % 2, a * P:(a + 1) * P]
                        mm = nc.tensor.matmul(half_of(o, lv, 1 - d), g, half_of(g, lv, 1 - d),
                                              start=True, stop=True)
                mm.then_inc(hg_pe.sem, 1)
                yield from pause(4 if lv else 3)

        def half_of(ap, lv, u):
            return ap.rearrange("p (n u h) -> p n u h", u=2, h=64 >> lv)[:, :, u, :]

        def hg_tensor_out(pe, turn, par):
            yield
            pe.wait_ge(hg_vec.sem, hg_vec.count("c6", turn))
            pe.wait_ge(hg_act.sem, hg_act.count("ao", turn))
            for h in range(2):
                for t in range(2):
                    o = ps[:, 0, (2 * h + t) * P:(2 * h + t + 1) * P]
                    nc.tensor.matmul(o, vn[:, 2 * h + t, :], AD[:, 2 * h + t, :], start=True, stop=False)
                    mm = nc.tensor.matmul(o, vn[:, 2 * h + 1 - t, :], AO[:, 1 - t, h, :], start=False,
                                          stop=True)
            mm.then_inc(hg_pe_out.sem, 1)
            yield from pause(2)
            pe.wait_ge(hg_act_out.sem, hg_act_out.count("osq", turn))
            nc.tensor.matmul(ps[:, 2, :], ones, out_sq, start=True, stop=True).then_inc(hg_pe_out.sem, 1)

        def hg_stage(eng, what, turn_expr, par, side):
            lap, g = BLOCK_AT["hg"] // SLOTS + 5 * turn_expr, GROUP_AT["hg"] + 5 * turn_expr
            for k in range(20):
                grp, kb = divmod(k, 4)
                gp = (par + grp) % 2
                if what == "act":
                    round_hi(eng, lap, k + AHEAD)
                    next(side, None)
                    if kb == 3:
                        copy_half(eng, lap, k, g + grp, gp)
                elif what == "dve":
                    take_lo(eng, lap, k + AHEAD)
                    next(side, None)
                    if kb == 3:
                        evacuate(eng, hin[:, par, grp].rearrange("p (h t) -> p h t", h=2), g + grp, gp)
                else:
                    multiply(eng, lap, k, g + grp, gp, hs, kb, 0, 3, side)
            drain(side)

        def hg_all(eng, what, take_in, attend, put_out):
            n = 2 if what == "pe" else 1
            hg_stage(eng, what, 0, 0, slots(20 * n, take_in(eng, 0, 0)))
            hg_stage(eng, what, 1, 1, slots(20 * n, attend(eng, 0, 0), take_in(eng, 1, 1)))
            with eng.Fori(0, 3) as i:
                hg_stage(eng, what, 2 * i + 2, 0, slots(20 * n, put_out(eng, 2 * i, 0),
                                                        attend(eng, 2 * i + 1, 1),
                                                        take_in(eng, 2 * i + 2, 0)))
                hg_stage(eng, what, 2 * i + 3, 1, slots(20 * n, put_out(eng, 2 * i + 1, 1),
                                                        attend(eng, 2 * i + 2, 0),
                                                        take_in(eng, 2 * i + 3, 1)))

            def last_turn():
                yield from slots(20 * n, put_out(eng, 6, 0), attend(eng, 7, 1))
                yield from put_out(eng, 7, 1)

            if what == "pe":
                eng.wait_ge(hg_vec_out.sem, hg_vec_out.count("lo", 5))
            split_product(eng, what, "hgout", os_, 0, last_turn())

        def gate_scalar(act):
            act.wait_ge(gate_in, 32)
            nc.scalar.activation(tls[:, 0], tl[:], ACT.Copy).then_inc(gt_act.sem, 1)
            nc.scalar.activation(ea[:], gaw[:, 0:8], ACT.Exp).then_inc(gt_act.sem, 1)
            act.wait_ge(gt_vec.sem, gt_vec.count("a"))
            lg = ps[:, 0, 0:32].rearrange("p (c n) -> p c n", c=2)
            nc.scalar.activation(gts[:, :, 0:8], lg[:, :, 0:8], ACT.Sigmoid).then_inc(gt_act.sem, 1)
            nc.scalar.activation(gt2[:, 1], gt2[:, 0], ACT.Abs).then_inc(gt_act.sem, 1)
            act.wait_ge(gt_act.sem, gt_act.count("abs"))
            nc.scalar.activation(gt2[:, 1], gt2[:, 1], ACT.Exp, scale=-1.0).then_inc(gt_act.sem, 1)
            act.wait_ge(gt_act.sem, gt_act.count("e"))
            nc.scalar.activation(gt2[:, 1], gt2[:, 1], ACT.Ln, bias=1.0).then_inc(gt_act.sem, 1)
            act.wait_ge(gt_vec.sem, gt_vec.count("cum"))
            nc.scalar.activation(gt2[:, 2], gt2[:, 3], ACT.Exp).then_inc(gt_act.sem, 1)
            act.wait_ge(gt_vec.sem, gt_vec.count("tot"))
            nc.scalar.activation(gt2[:, 4], gt2[:, 4], ACT.Exp).then_inc(gt_act.sem, 1)

        def gate_vector(dve):
            dve.wait_ge(gt_act.sem, gt_act.count("tlh"))
            nc.vector.tensor_tensor(tls[:, 1], tl[:], tls[:, 0].bitcast(F32), ALU.subtract).then_inc(gt_vec.sem, 1)
            dve.wait_ge(gt_pe.sem, gt_pe.count("lg"))
            lg = ps[:, 0, 0:32].rearrange("p (c n) -> p c n", c=2)
            nc.vector.tensor_tensor(
                gt2[:, 0], lg[:, :, 8:16], gaw[:, 8:16].unsqueeze(1).broadcast_to([P, 2, 8]), ALU.add).then_inc(gt_vec.sem, 1)
            dve.wait_ge(gt_act.sem, gt_act.count("l"))
            nc.vector.scalar_tensor_tensor(gt2[:, 2], gt2[:, 0], 0.0, gt2[:, 1], ALU.max,
                                                       ALU.add).then_inc(gt_vec.sem, 1)
            dve.wait_ge(gt_vec.sem, gt_vec.count("sp"))
            nc.vector.scalar_tensor_tensor(
                gts[:, :, 8:16], gt2[:, 2], -1.0, ea[:].unsqueeze(1).broadcast_to([P, 2, 8]),
                ALU.mult, ALU.mult).then_inc(gt_vec.sem, 1)
            dve.wait_ge(gt_pe.sem, gt_pe.count("cum"))
            nc.vector.tensor_copy(gt2[:, 3].rearrange("p c n -> p (c n)"), ps[:, 1, 0:16]).then_inc(gt_vec.sem, 1)
            dve.wait_ge(gt_vec.sem, gt_vec.count("cum"))
            nc.vector.tensor_tensor(gt2[:, 4].rearrange("p c n -> p (c n)"), ps[:, 1, 16:32],
                                                gt2[:, 3].rearrange("p c n -> p (c n)"), ALU.subtract).then_inc(gt_vec.sem, 1)
            dve.wait_ge(gt_act.sem, gt_act.count("egc"))
            nc.vector.tensor_tensor(gt2[:, 5], gt2[:, 2], gts[:, :, 0:8], ALU.mult).then_inc(gt_vec.sem, 1)

        def gate_tensor(pe):
            pe.wait_ge(gt_vec.sem, gt_vec.count("tll"))
            for c in range(2):
                o = ps[:, 0, 16 * c:16 * c + 16]
                for kt in range(DT):
                    hi = hs[:, kt, c * P:(c + 1) * P]
                    nc.tensor.matmul(o, hi, tls[:, 0, kt, :], start=(kt == 0), stop=False)
                    nc.tensor.matmul(o, hi, tls[:, 1, kt, :], start=False, stop=False)
                    mm = nc.tensor.matmul(o, hs[:, kt, T + c * P:T + (c + 1) * P], tls[:, 0, kt, :],
                                          start=False, stop=(kt == DT - 1))
            mm.then_inc(gt_pe.sem, 1)
            pe.wait_ge(gt_vec.sem, gt_vec.count("g"))
            for c in range(2):
                nc.tensor.matmul(ps[:, 1, 8 * c:8 * c + 8], row_le, gts[:, c, 8:16], start=True, stop=True)
                mm = nc.tensor.matmul(ps[:, 1, 16 + 8 * c:24 + 8 * c], ones, gts[:, c, 8:16], start=True,
                                      stop=True)
            mm.then_inc(gt_pe.sem, 1)

        def mix_stage(eng, what, first, groups, dest, side):
            for k in range(4 * groups):
                grp, kb = divmod(k, 4)
                k_, g = 4 * first + k, GROUP_AT["mix"] + first + grp
                lap, par = BLOCK_AT["mix"] // SLOTS, g % 2
                if what == "act":
                    round_hi(eng, lap, k_ + AHEAD)
                    next(side, None)
                    if kb == 3:
                        copy_half(eng, lap, k_, g, par)
                elif what == "dve":
                    take_lo(eng, lap, k_ + AHEAD)
                    next(side, None)
                    if kb == 3:
                        evacuate(eng, dest(grp), g, par)
                else:
                    multiply(eng, lap, k_, g, par, hs, kb, 0, 3, side)
            drain(side)

        def sb_tensor(pe, t, par):
            pe.wait_ge(evac, GROUP_AT["mix"] + 3 * t + 2 + 3)
            if t == 0:
                pe.wait_ge(gt_vec.sem, gt_vec.count("tot"))
            else:
                pe.wait_ge(sb_vec.sem, sb_vec.count("lo", t - 1))
            q, k, v = (sin[:, par, s] for s in range(3))
            for h in range(2):
                nc.tensor.matmul(ps[:, h, 0:T], k[:, h * T:h * T + P], q[:, h * T:(h + 1) * T],
                                 start=True, stop=True)
                nc.tensor.matmul(ps[:, h, T:T + P], k[:, h * T + P:(h + 1) * T],
                                 q[:, h * T + P:(h + 1) * T], start=True, stop=True)
            for a in range(4):
                mm = nc.tensor.transpose(ps[:, 2, a * P:(a + 1) * P], v[:, a * P:(a + 1) * P], ident)
            mm.then_inc(sb_pe.sem, 1)
            yield from pause(7)
            pe.wait_ge(sb_vec.sem, sb_vec.count("sp", t))
            for h in range(2):
                nc.tensor.matmul(ps[:, h, 0:T], row_ge, sp_[:, h, 0:T], start=True, stop=False)
                nc.tensor.matmul(ps[:, h, P:T], ones, sp_[:, h, T:T + P], start=False, stop=True)
                mm = nc.tensor.matmul(ps[:, h, T:T + P], row_ge, sp_[:, h, T:T + P], start=True, stop=True)
            mm.then_inc(sb_pe.sem, 1)
            yield from pause(5)
            pe.wait_ge(sb_act.sem, sb_act.count("w", t))
            for h in range(2):
                nc.tensor.matmul(ps[:, 3, h * T:(h + 1) * T], svn[:, 2 * h, :], se[:, h, 0:T],
                                 start=True, stop=False)
                mm = nc.tensor.matmul(ps[:, 3, h * T + P:(h + 1) * T], svn[:, 2 * h + 1, :],
                                      se[:, h, T:T + P], start=False, stop=True)
            mm.then_inc(sb_pe.sem, 1)

        def sb_scalar(act, t, par):
            yield
            act.wait_ge(sb_pe.sem, sb_pe.count("z", t))
            nc.scalar.activation(svn[:].rearrange("p a b -> p (a b)"), ps[:, 2, :], ACT.Copy).then_inc(sb_act.sem, 1)
            act.wait_ge(sb_vec.sem, sb_vec.count("zm", t))
            nc.scalar.activation(se[:], zm[:], ACT.Abs).then_inc(sb_act.sem, 1)
            act.wait_ge(sb_act.sem, sb_act.count("abs", t))
            nc.scalar.activation(se[:], se[:], ACT.Exp, scale=-1.0).then_inc(sb_act.sem, 1)
            act.wait_ge(sb_act.sem, sb_act.count("e", t))
            nc.scalar.activation(se[:], se[:], ACT.Ln, bias=1.0).then_inc(sb_act.sem, 1)
            yield
            yield
            yield
            act.wait_ge(sb_vec.sem, sb_vec.count("w", t))
            nc.scalar.activation(se[:], zm[:], ACT.Exp).then_inc(sb_act.sem, 1)
            yield
            yield
            act.wait_ge(sb_pe.sem, sb_pe.count("o", t))
            nc.scalar.activation(mixs[:, 2 * t:2 * t + 2, 0:T],
                                             ps[:, 3, :].rearrange("p (h n) -> p h n", h=2), ACT.Copy).then_inc(sb_act.sem, 1)

        def sb_vector(dve, t, par):
            yield
            dve.wait_ge(sb_pe.sem, sb_pe.count("z", t))
            if t == 0:
                dve.wait_ge(neg_in, 16)
            nc.vector.scalar_tensor_tensor(
                zm[:], ps[:, 0:2, 0:384], float(P) ** -0.5, neg[:].unsqueeze(1).broadcast_to([P, 2, 384]),
                ALU.mult, ALU.add).then_inc(sb_vec.sem, 1)
            yield
            dve.wait_ge(sb_act.sem, sb_act.count("l", t))
            nc.vector.scalar_tensor_tensor(sp_[:], zm[:], 0.0, se[:], ALU.max, ALU.add).then_inc(sb_vec.sem, 1)
            yield
            yield
            dve.wait_ge(sb_pe.sem, sb_pe.count("cs", t))
            nc.vector.tensor_tensor(zm[:], zm[:], ps[:, 0:2, 0:384], ALU.subtract).then_inc(sb_vec.sem, 1)
            yield
            yield
            dve.wait_ge(sb_act.sem, sb_act.count("hi", t))
            nc.vector.tensor_tensor(
                mixs[:, 2 * t:2 * t + 2, T:2 * T], ps[:, 3, :].rearrange("p (h n) -> p h n", h=2),
                mixs[:, 2 * t:2 * t + 2, 0:T].bitcast(F32), ALU.subtract).then_inc(sb_vec.sem, 1)

        def col(a):
            return slice(a * P, (a + 1) * P)

        def gd_vector(dve, t, par):
            dve.wait_ge(evac, GROUP_AT["mix"] + 12 + 4 * t + 3 + 3)
            if t == 0:
                dve.wait_ge(gpad_set, 1)
            for j in range(4):
                for s in range(3):
                    for h in range(2):
                        c = VEC_AT["gdn_conv"] + (s * 8 + 2 * t + h) * 4 + j
                        y, src = gy[:, s, h * T:(h + 1) * T], gin[:, par, s, h, j:j + T]
                        if j == 0:
                            ins = nc.vector.tensor_scalar(y, src, vec[:, c:c + 1], None, ALU.mult)
                        else:
                            dve.wait_ge(gd_vec.sem, gd_vec.count(f"c{j - 1}", t))
                            ins = nc.vector.scalar_tensor_tensor(y, src, vec[:, c:c + 1], y, ALU.mult, ALU.add)
                ins.then_inc(gd_vec.sem, 1)
                if j == 1:
                    yield
            yield
            for h in range(2):
                for c in range(2):
                    ins = nc.vector.tensor_scalar(gbm[:, 2 * h + c, :], ones, gts[:, c, 8 + 2 * t + h:9 + 2 * t + h],
                                                  None, ALU.mult)
            ins.then_inc(gd_vec.sem, 1)
            for h in range(2):
                for c in range(2):
                    ins = nc.vector.tensor_scalar(bbm[:, 2 * h + c, :], ones, gts[:, c, 2 * t + h:1 + 2 * t + h],
                                                  -1.0, ALU.mult, ALU.mult)
            ins.then_inc(gd_vec.sem, 1)
            yield from pause(2)
            dve.wait_ge(gd_act.sem, gd_act.count("r", t))
            nc.vector.scalar_tensor_tensor(gy[:, 0], gy[:, 0], float(P) ** -0.5, gr[:, 0:2 * T],
                                                       ALU.mult, ALU.mult).then_inc(gd_vec.sem, 1)
            nc.vector.tensor_tensor(gy[:, 1], gy[:, 1], gr[:, 2 * T:4 * T], ALU.mult).then_inc(gd_vec.sem, 1)
            dve.wait_ge(gd_pe.sem, gd_pe.count("rows", t))
            for h in range(2):
                for c in range(2):
                    ins = nc.vector.tensor_scalar(DTr[:, 2 * h + c, :], ps[:, 2, col(2 * h + c)],
                                                  gt2[:, 3, c, 2 * t + h:2 * t + h + 1], 0.0,
                                                  ALU.subtract, ALU.min)
            ins.then_inc(gd_vec.sem, 1)
            yield
            yield
            flat = "p a b -> p (a b)"
            dve.wait_ge(gd_pe.sem, gd_pe.count("kk", t))
            dve.wait_ge(gd_act.sem, gd_act.count("dt", t))
            nc.vector.tensor_tensor(NLT[:].rearrange(flat), ps[:, 0, :], DTr[:].rearrange(flat),
                                                ALU.mult).then_inc(gd_vec.sem, 1)
            nc.vector.tensor_tensor(ATr[:].rearrange(flat), ps[:, 1, :], DTr[:].rearrange(flat),
                                                ALU.mult).then_inc(gd_vec.sem, 1)
            dve.wait_ge(gd_vec.sem, gd_vec.count("nl0", t))
            nc.vector.tensor_tensor(NLT[:].rearrange(flat), NLT[:].rearrange(flat), ps[:, 3, :],
                                                ALU.mult).then_inc(gd_vec.sem, 1)
            dve.wait_ge(gd_vec.sem, gd_vec.count("at0", t))
            nc.vector.tensor_tensor(ATr[:], ATr[:], row_le.unsqueeze(1).broadcast_to([P, 4, P]),
                                                ALU.mult).then_inc(gd_vec.sem, 1)
            q1 = gy[:, 0].rearrange("p (h c n) -> p h c n", h=2, c=2)[:, :, 1, :]
            nc.vector.tensor_tensor(qd[:], qd[:], q1, ALU.mult).then_inc(gd_vec.sem, 1)
            nc.vector.tensor_copy(Tm[:], ident.unsqueeze(1).broadcast_to([P, 4, P])).then_inc(gd_vec.sem, 1)
            nc.vector.memset(Y[:], 0.0)
            nc.vector.tensor_copy(TT[:], ident.unsqueeze(1).broadcast_to([P, 4, P])).then_inc(gd_vec.sem, 1)
            yield
            for lv in range(LEVELS):
                dve.wait_ge(gd_pe.sem, gd_pe.count(f"z{lv}", t))
                if lv == 0:
                    dve.wait_ge(gd_vec.sem, gd_vec.count("TT", t))
                else:
                    dve.wait_ge(gd_vec.sem, gd_vec.count(f"tt{lv - 1}", t))
                m_ = msk[:, LEVELS - 1 - lv, :]
                for u, (to, w) in enumerate(((Tm, "t"), (TT, "tt"))):
                    dve.sem_inc(copies_begun, 1)
                    nc.vector.copy_predicated(
                        half4(to[:].rearrange(flat), lv, u),
                        half_of(m_, LEVELS - 1 - lv, u).unsqueeze(1).broadcast_to(
                            [P, 4, 64 >> lv, 1 << lv]),
                        half4(ps[:, 1, :], lv, u)).then_inc(gd_vec.sem, 1)
                yield
            yield
            dve.wait_ge(gd_pe.sem, gd_pe.count("S", t))
            nc.vector.tensor_copy(Sm[:].rearrange(flat), ps[:, 2, 0:2 * P]).then_inc(gd_vec.sem, 1)

        def half4(ap, lv, u):
            return ap.rearrange("p (a n u h) -> p a n u h", a=4, u=2, h=1 << lv)[:, :, :, u, :]

        o_sq, o_rms, o_out = (b[:].rearrange("p a b -> p (a b)") for b in (NLT, Tm, Y))

        def gd_vector_out(dve, t, par):
            yield from pause(2)
            dve.wait_ge(gd_act_out.sem, gd_act_out.count("or", t))
            og, gain = o_out, vec[:, VEC_AT["gdn_gain"]:VEC_AT["gdn_gain"] + 1]
            nc.vector.scalar_tensor_tensor(og, ps[:, 0, :], gain, o_rms, ALU.mult,
                                                       ALU.mult).then_inc(gd_vec_out.sem, 1)
            dve.wait_ge(gd_vec_out.sem, gd_vec_out.count("og", t))
            o2 = og.rearrange("p (h n) -> p h n", h=2)
            nc.vector.tensor_tensor(o2, o2, gin[:, par, 3, :, 3:3 + T], ALU.mult).then_inc(gd_vec_out.sem, 1)
            dve.wait_ge(gd_vec_out.sem, gd_vec_out.count("os", t))
            dst = mixs[:, 8 + 2 * t:10 + 2 * t, :]
            nc.vector.tensor_scalar(dst[:, :, 0:T], o2, 1.0, None, ALU.mult).then_inc(gd_vec_out.sem, 1)
            dve.wait_ge(gd_vec_out.sem, gd_vec_out.count("hi", t))
            nc.vector.tensor_tensor(dst[:, :, T:2 * T], o2, dst[:, :, 0:T].bitcast(F32),
                                                ALU.subtract).then_inc(gd_vec_out.sem, 1)

        def gd_scalar(act, t, par):
            flat = "p a b -> p (a b)"
            yield
            yield
            act.wait_ge(gd_vec.sem, gd_vec.count("c3", t))
            nc.scalar.activation(gin[:, par, 3, :, 3:3 + T], gin[:, par, 3, :, 3:3 + T], ACT.Silu)
            nc.scalar.activation(gy[:], gy[:], ACT.Silu).then_inc(gd_act.sem, 1)
            act.wait_ge(gd_act.sem, gd_act.count("silu", t))
            nc.scalar.activation(gs[:], gy[:, 0:2, :].rearrange("p a b -> p (a b)"), ACT.Square).then_inc(gd_act.sem, 1)
            yield
            yield
            act.wait_ge(gd_pe.sem, gd_pe.count("ssq", t))
            nc.scalar.activation(gr[:].rearrange("p (a b) -> p a b", a=2), ps[:, 0:2, :], ACT.Ln,
                                             bias=EPS).then_inc(gd_act.sem, 1)
            act.wait_ge(gd_act.sem, gd_act.count("ln", t))
            nc.scalar.activation(gr[:], gr[:], ACT.Exp, scale=-0.5).then_inc(gd_act.sem, 1)
            rows = ps[:, 2, :].rearrange("p (h c n) -> p h c n", h=2, c=2)
            act.wait_ge(gd_vec.sem, gd_vec.count("d", t))
            nc.scalar.activation(qd[:], rows[:, :, 1, :], ACT.Exp).then_inc(gd_act.sem, 1)
            nc.scalar.activation(DTr[:], DTr[:], ACT.Exp).then_inc(gd_act.sem, 1)
            yield
            yield
            yield
            act.wait_ge(gd_pe.sem, gd_pe.count("tr", t))
            for h in range(2):
                for c in range(2):
                    ins = nc.scalar.activation(vb[:, 2 * h + c, :], ps[:, 3, col(2 * h + c)], ACT.Copy,
                                               scale=gts[:, c, 2 * t + h:2 * t + h + 1])
            ins.then_inc(gd_act.sem, 1)
            for h in range(2):
                ins = nc.scalar.activation(kbe[:, h, :], ps[:, 2, col(2 * h + 1)], ACT.Copy,
                                           scale=gt2[:, 5, 1, 2 * t + h:2 * t + h + 1])
            ins.then_inc(gd_act.sem, 1)
            for h in range(2):
                ins = nc.scalar.activation(ktl[:, h, :], ps[:, 2, col(2 * h)], ACT.Copy,
                                           scale=gt2[:, 4, 0, 2 * t + h:2 * t + h + 1])
            ins.then_inc(gd_act.sem, 1)
            for lv in range(LEVELS):
                act.wait_ge(gd_pe.sem, gd_pe.count(f"y{lv}", t))
                nc.scalar.activation(half4(Y[:].rearrange(flat), lv, 0), half4(ps[:, 0, :], lv, 0),
                                                 ACT.Copy).then_inc(gd_act.sem, 1)
                yield
            act.wait_ge(gd_pe.sem, gd_pe.count("uw", t))
            nc.scalar.activation(u0[:].rearrange(flat), ps[:, 0, 0:2 * P], ACT.Copy).then_inc(gd_act.sem, 1)
            nc.scalar.activation(nwT[:].rearrange(flat), ps[:, 1, 0:2 * P], ACT.Copy,
                                             scale=-1.0).then_inc(gd_act.sem, 1)

        def gd_scalar_out(act, t, par):
            flat = "p a b -> p (a b)"
            act.wait_ge(gd_pe_out.sem, gd_pe_out.count("vn", t))
            nc.scalar.activation(vnw[:].rearrange(flat), ps[:, 3, 0:2 * P], ACT.Copy).then_inc(gd_act_out.sem, 1)
            yield
            act.wait_ge(gd_pe_out.sem, gd_pe_out.count("o", t))
            nc.scalar.activation(o_sq, ps[:, 0, :], ACT.Square).then_inc(gd_act_out.sem, 1)
            yield
            act.wait_ge(gd_pe_out.sem, gd_pe_out.count("os", t))
            nc.scalar.activation(o_rms, ps[:, 1, :], ACT.Ln, bias=EPS, scale=1.0 / P).then_inc(gd_act_out.sem, 1)
            act.wait_ge(gd_act_out.sem, gd_act_out.count("oln", t))
            nc.scalar.activation(o_rms, o_rms, ACT.Exp, scale=-0.5).then_inc(gd_act_out.sem, 1)

        def gd_tensor(pe, t, par):
            yield from pause(7)
            pe.wait_ge(gd_act.sem, gd_act.count("sqk", t))
            if t == 0:
                pe.wait_ge(sb_vec.sem, sb_vec.count("lo", 3))
            else:
                pe.wait_ge(gd_vec_out.sem, gd_vec_out.count("og", t - 1))
            for b in range(2):
                mm = nc.tensor.matmul(ps[:, b, :], ones, gs[:, b * 2 * T:(b + 1) * 2 * T], start=True, stop=True)
            mm.then_inc(gd_pe.sem, 1)
            pe.wait_ge(gd_vec.sem, gd_vec.count("bbm", t))
            for a in range(4):
                nc.tensor.matmul(ps[:, 2, col(a)], gbm[:, a, :], row_le, start=True, stop=True)
                mm = nc.tensor.matmul(ps[:, 3, col(a)], bbm[:, a, :], ident, start=True, stop=True)
            mm.then_inc(gd_pe.sem, 1)
            yield from pause(4)
            pe.wait_ge(gd_vec.sem, gd_vec.count("k", t))
            for a in range(4):
                nc.tensor.matmul(ps[:, 0, col(a)], gy[:, 1, col(a)], gy[:, 1, col(a)], start=True, stop=True)
                mm = nc.tensor.matmul(ps[:, 1, col(a)], gy[:, 1, col(a)], gy[:, 0, col(a)], start=True, stop=True)
            mm.then_inc(gd_pe.sem, 1)
            yield from pause(2)
            pe.wait_ge(gd_vec.sem, gd_vec.count("TT", t))
            pe.wait_ge(gd_act.sem, gd_act.count("qe", t))
            for a in range(4):
                nc.tensor.transpose(ps[:, 2, col(a)], gy[:, 1, col(a)], ident)
                mm = nc.tensor.transpose(ps[:, 3, col(a)], gy[:, 2, col(a)], ident)
            mm.then_inc(gd_pe.sem, 1)
            yield
            for lv in range(LEVELS):
                if lv:
                    pe.wait_ge(gd_vec.sem, gd_vec.count(f"tt{lv - 1}", t))
                for a in range(4):
                    mm = nc.tensor.matmul(half_of(ps[:, 0, col(a)], LEVELS - 1 - lv, 0), NLT[:, a, :],
                                          half_of(Tm[:, a, :], LEVELS - 1 - lv, 0), start=True, stop=True)
                mm.then_inc(gd_pe.sem, 1)
                yield
                pe.wait_ge(gd_act.sem, gd_act.count(f"y{lv}", t))
                for a in range(4):
                    y, tt = Y[:, a, :], TT[:, a, :]
                    nc.tensor.matmul(half_of(ps[:, 1, col(a)], LEVELS - 1 - lv, 0), tt,
                                     half_of(y, LEVELS - 1 - lv, 0), start=True, stop=True)
                    mm = nc.tensor.matmul(half_of(ps[:, 1, col(a)], LEVELS - 1 - lv, 1), y,
                                          half_of(tt, LEVELS - 1 - lv, 1), start=True, stop=True)
                mm.then_inc(gd_pe.sem, 1)
                yield
            pe.wait_ge(gd_vec.sem, gd_vec.count(f"tt{LEVELS - 1}", t))
            pe.wait_ge(gd_act.sem, gd_act.count("ktl", t))
            for h in range(2):
                nc.tensor.matmul(ps[:, 0, col(h)], TT[:, 2 * h, :], vb[:, 2 * h, :], start=True, stop=True)
                mm = nc.tensor.matmul(ps[:, 1, col(h)], kbe[:, h, :], TT[:, 2 * h + 1, :], start=True, stop=True)
            mm.then_inc(gd_pe.sem, 1)
            yield
            pe.wait_ge(gd_act.sem, gd_act.count("nw", t))
            for h in range(2):
                mm = nc.tensor.matmul(ps[:, 2, col(h)], ktl[:, h, :], u0[:, h, :], start=True, stop=True)
            mm.then_inc(gd_pe.sem, 1)

        def gd_tensor_out(pe, t, par):
            pe.wait_ge(gd_vec.sem, gd_vec.count("S", t))
            for h in range(2):
                nc.tensor.matmul(ps[:, 3, col(h)], TT[:, 2 * h + 1, :], vb[:, 2 * h + 1, :], start=True, stop=False)
                mm = nc.tensor.matmul(ps[:, 3, col(h)], nwT[:, h, :], Sm[:, h, :], start=False, stop=True)
            mm.then_inc(gd_pe_out.sem, 1)
            yield
            pe.wait_ge(gd_act_out.sem, gd_act_out.count("vn", t))
            for h in range(2):
                nc.tensor.matmul(ps[:, 0, col(2 * h)], u0[:, h, :], ATr[:, 2 * h, :], start=True, stop=True)
                nc.tensor.matmul(ps[:, 0, col(2 * h + 1)], vnw[:, h, :], ATr[:, 2 * h + 1, :], start=True, stop=False)
                mm = nc.tensor.matmul(ps[:, 0, col(2 * h + 1)], Sm[:, h, :], qd[:, h, :], start=False, stop=True)
            mm.then_inc(gd_pe_out.sem, 1)
            yield from pause(2)
            pe.wait_ge(gd_act_out.sem, gd_act_out.count("osq", t))
            nc.tensor.matmul(ps[:, 1, :], ones, o_sq, start=True, stop=True).then_inc(gd_pe_out.sem, 1)

        def mix_all(eng, what, attend, delta, put_out):
            n = 2 if what == "pe" else 1

            def qkv(par):
                return lambda s: sin[:, par, s].rearrange("p (h n) -> p h n", h=2)

            def qkvz(par):
                return lambda s: gin[:, par, s, :, 3:3 + T]

            for t in range(4):
                mix_stage(eng, what, 3 * t, 3, qkv(t % 2), attend(eng, t - 1, (t - 1) % 2) if t else pause(0))
            for t in range(4):
                if t == 0:
                    side = attend(eng, 3, 1)
                elif t == 1:
                    side = slots(16 * n, delta(eng, 0, 0))
                else:
                    side = slots(16 * n, put_out(eng, t - 2, t % 2), delta(eng, t - 1, (t - 1) % 2))
                mix_stage(eng, what, 12 + 4 * t, 4, qkvz(t % 2), side)

            def last_turn():
                yield from slots(16 * n, put_out(eng, 2, 0), delta(eng, 3, 1))
                yield from put_out(eng, 3, 1)

            if what == "pe":
                eng.wait_ge(gd_vec_out.sem, gd_vec_out.count("lo", 1))
            split_product(eng, what, "mixout", mixs, 8, last_turn())

        def cross_tensor(pe):
            pe.wait_ge(evac, GROUP_AT["xq"] + 1 + 3)
            for h in range(4):
                for c in range(2):
                    mm = nc.tensor.matmul(ps[:, h, c * T:(c + 1) * T], xq[:, h, col(c)], kv[:, h, :],
                                          start=True, stop=True)
            mm.then_inc(xa_pe.sem, 1)
            pe.wait_ge(xa_act.sem, xa_act.count("p"))
            for h in range(4):
                for c in range(2):
                    mm = nc.tensor.transpose(ps[:, h // 2, (h % 2 * 2 + c) * P:(h % 2 * 2 + c + 1) * P],
                                             kv[:, 4 + h, col(c)], ident)
            mm.then_inc(xa_pe.sem, 1)
            pe.wait_ge(xa_act.sem, xa_act.count("vn"))
            pe.wait_ge(xa_vec.sem, xa_vec.count("p"))
            for h in range(4):
                for c in range(2):
                    for b in range(2):
                        mm = nc.tensor.transpose(ps[:, h, c * T + b * P:c * T + (b + 1) * P],
                                                 pr[:, 2 * h + b, col(c)], ident)
            mm.then_inc(xa_pe.sem, 1)
            pe.wait_ge(xa_act.sem, xa_act.count("pt"))
            for h in range(4):
                for c in range(2):
                    mm = nc.tensor.matmul(ps[:, h // 2, h % 2 * T:(h % 2 + 1) * T], xvn[:, h, c, :],
                                          prT[:, h, c, :], start=(c == 0), stop=(c == 1))
            mm.then_inc(xa_pe.sem, 1)

        def cross_scalar(act):
            act.wait_ge(xa_vec.sem, xa_vec.count("nmx"))
            for a in range(8):
                ins = nc.scalar.activation(pr[:, a, :], ps[:, a // 2, a % 2 * T:(a % 2 + 1) * T], ACT.Exp,
                                           bias=mx[:, a:a + 1], scale=float(P) ** -0.5, accum_out=sm[:, a:a + 1])
            ins.then_inc(xa_act.sem, 1)
            act.wait_ge(xa_pe.sem, xa_pe.count("vt"))
            nc.scalar.activation(xvn[:].rearrange("p h c n -> p (h c n)").rearrange(
                "p (a b) -> p a b", a=2), ps[:, 0:2, :], ACT.Copy).then_inc(xa_act.sem, 1)
            act.wait_ge(xa_pe.sem, xa_pe.count("pt"))
            nc.scalar.activation(prT[:].rearrange("p h c n -> p h (c n)"), ps[:], ACT.Copy).then_inc(xa_act.sem, 1)
            act.wait_ge(xa_pe.sem, xa_pe.count("o"))
            nc.scalar.activation(xs[:, :, 0:T], ps[:, 0:2, :].rearrange(
                "p a (b n) -> p (a b) n", b=2), ACT.Copy).then_inc(xa_act.sem, 1)

        def cross_vector(dve):
            dve.wait_ge(xa_pe.sem, xa_pe.count("z"))
            nc.vector.reduce_max(mx[:], ps[:].rearrange("p h (c n) -> p (h c) n", c=2), AXX).then_inc(xa_vec.sem, 1)
            dve.wait_ge(xa_vec.sem, xa_vec.count("mx"))
            nc.vector.tensor_scalar(mx[:], mx[:], -float(P) ** -0.5, None, ALU.mult).then_inc(xa_vec.sem, 1)
            dve.wait_ge(xa_act.sem, xa_act.count("p"))
            nc.vector.reciprocal(rs[:], sm[:]).then_inc(xa_vec.sem, 1)
            dve.wait_ge(xa_vec.sem, xa_vec.count("rs"))
            nc.vector.tensor_tensor(pr[:], pr[:], rs[:].unsqueeze(2).broadcast_to([P, 8, T]),
                                                ALU.mult).then_inc(xa_vec.sem, 1)
            dve.wait_ge(xa_act.sem, xa_act.count("hi"))
            nc.vector.tensor_tensor(xs[:, :, T:2 * T], ps[:, 0:2, :].rearrange(
                "p a (b n) -> p (a b) n", b=2), xs[:, :, 0:T].bitcast(F32), ALU.subtract).then_inc(xa_vec.sem, 1)

        def mlp(eng, what, which):
            name, cname = ("up1", "conv1") if which == 0 else ("up2", "conv2")
            first = 1 + which
            va, aa = mlp_vec[which], mlp_act[which]
            lap0, g0 = BLOCK_AT[name] // SLOTS, GROUP_AT[name]
            if what == "dve":
                nc.vector.memset(cin[:, :, 0:first], 0.0).then_inc(pad_set[which], 1)
                if which == 0:
                    nc.vector.memset(cin[:, :, T + 1:T + 2], 0.0).then_inc(pad_set[which], 1)
            with eng.Fori(0, UP_GROUPS // 2) as i:
                lap, g = lap0 + 2 * i, g0 + 2 * i
                for k in range(8):
                    part, kb = divmod(k, 4)
                    if what == "act":
                        round_hi(eng, lap, k + AHEAD)
                        if kb == 3:
                            copy_half(eng, lap, k, g + part, part)
                            if part == 0:
                                eng.wait_ge(va.sem, va.count("a21", i))
                                nc.scalar.activation(cy[:, 0:2, :], cy[:, 0:2, :], ACT.Silu).then_inc(aa.sem, 1)
                    elif what == "dve":
                        take_lo(eng, lap, k + AHEAD)
                        if kb == 3:
                            evacuate(eng, cin[:, 2 * part:2 * part + 2, first:first + T], g + part, part)
                            eng.wait_ge(evac, g + part + 3)
                            w = "ab"[part]
                            if part == 0:
                                eng.wait_ge(pad_set[which], 2 - which)
                            for tap in range(3):
                                for t in range(2):
                                    y, src = cy[:, 2 * part + t, :], cin[:, 2 * part + t, tap:tap + T]
                                    col = VEC_AT[cname] + (FT * part + 2 * i + t) * 4
                                    if tap == 0:
                                        ins = nc.vector.tensor_scalar(
                                            y, src, vec[:, bass.ds(col, 1)], vec[:, bass.ds(col + 3, 1)],
                                            ALU.mult, ALU.add)
                                    else:
                                        eng.wait_ge(va.sem, va.count(f"{w}{tap - 1}{t}", i))
                                        ins = nc.vector.scalar_tensor_tensor(
                                            y, src, vec[:, bass.ds(col + tap, 1)], y, ALU.mult, ALU.add)
                                    ins.then_inc(va.sem, 1)
                    else:
                        multiply(eng, lap, k, g + part, part, hs, kb, 0, 3)
                if what == "dve":
                    eng.wait_ge(aa.sem, aa.count("silu", i))
                    eng.wait_ge(va.sem, va.count("b21", i))
                    nc.vector.tensor_tensor(cy[:, 0:2, :], cy[:, 0:2, :], cy[:, 2:4, :], ALU.mult).then_inc(va.sem, 1)
                    eng.wait_ge(va.sem, va.count("mul", i))
                    dst = acts[:, bass.ds(2 * i, 2), :]
                    nc.vector.tensor_scalar(dst[:, :, 0:T], cy[:, 0:2, :], 1.0, None, ALU.mult).then_inc(va.sem, 1)
                    eng.wait_ge(va.sem, va.count("hi", i))
                    nc.vector.tensor_tensor(dst[:, :, T:2 * T], cy[:, 0:2, :],
                                                    dst[:, :, 0:T].bitcast(F32), ALU.subtract).then_inc(va.sem, 1)

        def x_ready(s):
            return lambda eng, c: eng.wait_ge(norm_vec.sem, norm_vec.count(f"{s}_x{c}"))

        def m_ready(name, first=0):
            return lambda eng, c: eng.wait_ge(evac, GROUP_AT[name] + first + 2 * c + 1 + 3)

        block = ctx.enter_context(nc.Block())

        @block.sync
        def _(sp):
            sp.dma_start(x[:], xT).then_inc(const_in, 16)
            sp.dma_start(vec[:], vecs).then_inc(const_in, 16)
            sp.dma_start(cst[:], consts[:, 0:4 * P].rearrange("p (a b) -> p a b", a=4)).then_inc(const_in, 16)
            sp.dma_start(G[:].rearrange("p a b -> p (a b)")[:, 0:LEVELS * P], masks).then_inc(const_in, 16)
            sp.dma_start(reset[:], consts[:, 4 * P:4 * P + 2 * T]).then_inc(const_in, 16)
            with sp.Fori(0, N_BLOCKS // SLOTS) as i:
                for b in range(SLOTS):
                    sp.wait_ge(lo_ready, SLOTS * i + b + 1)
                    sp.dma_start(raw[:, b, :], stream[SLOTS * i + b]).then_inc(raw_in[b], 16)

        @block.scalar
        def _(act):
            for s in (norm_act, hg_act_in, hg_act, hg_act_out, *mlp_act, gt_act, sb_act, gd_act, gd_act_out, xa_act):
                act.sem_inc(s.sem, 1)
            act.wait_ge(const_in, 80)
            for k in range(AHEAD):
                round_hi(act, 0, k)
            norm_scalar(act, "n1", "pre", x, lambda e, c: None)
            act.wait_ge(hg_set, 2)
            lb2 = lb[:].rearrange("p a b -> p (a b)")
            nc.scalar.activation(lb2, lb2, ACT.Exp).then_inc(hg_exp, 1)
            hg_all(act, "act", hg_scalar_in, hg_scalar, hg_scalar_out)
            norm_scalar(act, "n2", "post", m, m_ready("hgout", 8))
            norm_scalar(act, "n3", "pre", x, x_ready("n2"))
            mlp(act, "act", 0)
            product(act, "act", "down1", DOWN_BLOCKS, 2, 4)
            norm_scalar(act, "n4", "post", m, m_ready("down1"))
            norm_scalar(act, "n5", "pre", x, x_ready("n4"))
            gate_scalar(act)
            mix_all(act, "act", sb_scalar, gd_scalar, gd_scalar_out)
            norm_scalar(act, "n7", "pre", memr, lambda e, c: e.wait_ge(mem_in, 16), mems)
            product(act, "act", "kv", 4, 2, 2, dest=kv)
            norm_scalar(act, "n8", "pre", x, x_ready("n6"))
            product(act, "act", "xq", 4, 1, 2, dest=xq)
            cross_scalar(act)
            product(act, "act", "xo", 1, 2, 4)
            norm_scalar(act, "n10", "pre", x, x_ready("n9"))
            mlp(act, "act", 1)
            product(act, "act", "down2", DOWN_BLOCKS, 2, 4, last=True)
            norm_scalar(act, "n12", "final", x, x_ready("n11"))

        @block.vector
        def _(dve):
            for s in (norm_vec, hg_vec_in, hg_vec, hg_vec_out, *mlp_vec, gt_vec, sb_vec, gd_vec, gd_vec_out, xa_vec):
                dve.sem_inc(s.sem, 1)
            dve.sem_inc(lo_ready, SLOTS)
            dve.sem_inc(evac, 2)
            dve.wait_ge(const_in, 80)
            for k in range(AHEAD):
                take_lo(dve, 0, k)
            norm_pre_vector(dve, "n1", "pre_mix", hs)
            bnd = vec[:, VEC_AT["bounds"]:VEC_AT["bounds"] + 2 * HEADS]
            lb2, oml2 = lb[:].rearrange("p a b -> p (a b)"), oml[:].rearrange("p a b -> p (a b)")
            nc.vector.tensor_copy(msk[:].rearrange("p l n -> p (l n)"),
                                  G[:].rearrange("p a b -> p (a b)")[:, 0:LEVELS * P])
            nc.vector.memset(lf[:, 0:1], 0.0).then_inc(hg_set, 1)
            nc.vector.tensor_tensor(lb2, bnd, bnd, ALU.subtract).then_inc(hg_set, 1)
            dve.wait_ge(hg_exp, 1)
            nc.vector.reciprocal(oml2, lb2).then_inc(hg_set, 1)
            dve.wait_ge(hg_set, 3)
            nc.vector.tensor_tensor(lb2, lb2, oml2, ALU.mult).then_inc(hg_set, 1)
            dve.wait_ge(hg_set, 4)
            nc.vector.tensor_tensor(lb2, lb2, lb2, ALU.subtract).then_inc(hg_set, 1)
            dve.wait_ge(hg_set, 5)
            nc.vector.tensor_scalar(oml2, lb2, -1.0, 1.0, ALU.mult, ALU.add).then_inc(hg_set, 1)
            dve.wait_ge(hg_set, 6)
            hg_all(dve, "dve", hg_vector_in, hg_vector, hg_vector_out)
            norm_post_vector(dve, "n2", "post_mix")
            norm_pre_vector(dve, "n3", "pre_ffn", hs)
            mlp(dve, "dve", 0)
            product(dve, "dve", "down1", DOWN_BLOCKS, 2, 4)
            norm_post_vector(dve, "n4", "post_ffn")
            norm_pre_vector(dve, "n5", "mix", hs)
            gate_vector(dve)
            nc.vector.memset(gin[:, :, :, :, 0:3], 0.0).then_inc(gpad_set, 1)
            mix_all(dve, "dve", sb_vector, gd_vector, gd_vector_out)
            add_vector(dve, "n6", "mixout", 8)
            norm_pre_vector(dve, "n7", "mem", mems, memr)
            product(dve, "dve", "kv", 4, 2, 2, dest=kv)
            norm_pre_vector(dve, "n8", "xattn", hs)
            product(dve, "dve", "xq", 4, 1, 2, dest=xq)
            cross_vector(dve)
            product(dve, "dve", "xo", 1, 2, 4)
            add_vector(dve, "n9", "xo")
            norm_pre_vector(dve, "n10", "ffn2", hs)
            mlp(dve, "dve", 1)
            product(dve, "dve", "down2", DOWN_BLOCKS, 2, 4, last=True)
            add_vector(dve, "n11", "down2")
            norm_pre_vector(dve, "n12", "final", None)

        @block.tensor
        def _(pe):
            for s in (norm_pe, hg_pe, hg_pe_out, gt_pe, sb_pe, gd_pe, gd_pe_out, xa_pe):
                pe.sem_inc(s.sem, 1)
            pe.sem_inc(blk_used, SLOTS)
            pe.wait_ge(const_in, 80)
            norm_tensor(pe, "n1")
            pe.wait_ge(norm_vec.sem, norm_vec.count("n1_lo3"))
            hg_all(pe, "pe", lambda *a: pause(0), hg_tensor, hg_tensor_out)
            norm_tensor(pe, "n2")
            norm_tensor(pe, "n3")
            pe.wait_ge(norm_vec.sem, norm_vec.count("n3_lo3"))
            mlp(pe, "pe", 0)
            pe.wait_ge(mlp_vec[0].sem, mlp_vec[0].count("lo", UP_GROUPS // 2 - 1))
            product(pe, "pe", "down1", DOWN_BLOCKS, 2, 4, acts)
            norm_tensor(pe, "n4")
            norm_tensor(pe, "n5")
            pe.wait_ge(norm_vec.sem, norm_vec.count("n5_lo3"))
            gate_tensor(pe)
            mix_all(pe, "pe", sb_tensor, gd_tensor, gd_tensor_out)
            norm_tensor(pe, "n7")
            pe.wait_ge(norm_vec.sem, norm_vec.count("n7_lo3"))
            product(pe, "pe", "kv", 4, 2, 2, mems, dest=kv)
            norm_tensor(pe, "n8")
            pe.wait_ge(norm_vec.sem, norm_vec.count("n8_lo3"))
            product(pe, "pe", "xq", 4, 1, 2, hs)
            cross_tensor(pe)
            pe.wait_ge(xa_vec.sem, xa_vec.count("lo"))
            product(pe, "pe", "xo", 1, 2, 4, xs)
            norm_tensor(pe, "n10")
            pe.wait_ge(norm_vec.sem, norm_vec.count("n10_lo3"))
            mlp(pe, "pe", 1)
            pe.wait_ge(mlp_vec[1].sem, mlp_vec[1].count("lo", UP_GROUPS // 2 - 1))
            product(pe, "pe", "down2", DOWN_BLOCKS, 2, 4, acts, last=True)
            norm_tensor(pe, "n12")

        @block.gpsimd
        def _(pool):
            pool.wait_ge(evac, GROUP_AT["down1"] + 7 + 3)
            pool.dma_start(tl[:], tail).then_inc(gate_in, 16)
            pool.dma_start(gaw[:], gates).then_inc(gate_in, 16)
            pool.dma_start(neg[:], consts[:, 4 * P + 2 * T:4 * P + 2 * T + 384]).then_inc(neg_in, 16)
            pool.wait_ge(gd_vec_out.sem, gd_vec_out.count("lo", 3))
            pool.wait_ge(gd_act_out.sem, gd_act_out.count("or", 3))
            pool.wait_ge(gd_pe_out.sem, gd_pe_out.count("os", 3))
            pool.dma_start(memr[:], memT).then_inc(mem_in, 16)
            pool.wait_ge(norm_vec.sem, norm_vec.count("n12_h3"))
            pool.dma_start(outT, sq[:]).then_inc(out_done, 16)
            pool.wait_ge(out_done, 16)


def tiles(a):
    return a.reshape(a.shape[0] // P, P, *a.shape[1:]).swapaxes(0, 1)


def blocks(w, order=None):
    k, n = w.shape
    a = w.reshape(k // 512, 4, P, n // 256, 256).transpose(3, 0, 2, 1, 4)
    if order is not None:
        a = a[np.array(order)]
    return a.reshape(-1, P, BLK)


def last_rows_last(b):
    b = b.reshape(8, 4, P, BLK)
    return np.concatenate([b[:, :3].reshape(24, P, BLK), b[:, 3]])


def lay_out(i):
    f32 = np.float32
    per_turn = [s * 8 + t for t in range(8) for s in (1, 2, 0, 4, 3)]
    per_pair = [s * (F // 256) + t for t in range(F // 256) for s in range(2)]
    mix = [s * 4 + t for t in range(4) for s in (0, 1, 2)]
    mix += [s * 4 + t for t in range(4) for s in (3, 4, 5, 6)]
    w_in2 = i["w_in_2"][0]
    stream = np.concatenate([
        blocks(i["hgrn_w_in"][0], per_turn), last_rows_last(blocks(i["hgrn_w_out"][0])),
        blocks(i["ffn_w_in"][0], per_pair), blocks(i["ffn_w_out"][0]),
        blocks(w_in2[:, :28 * 256], mix), last_rows_last(blocks(i["w_out_2"][0])), blocks(i["w_xkv_2"][0]),
        blocks(i["w_xq_2"][0]), blocks(i["w_xo_2"][0]), blocks(i["w_up_2"][0], per_pair),
        blocks(i["w_down_2"][0])])
    assert len(stream) == N_BLOCKS
    cols = lambda v: v.reshape(-1, P).T
    taps = lambda rows: tiles(np.stack(rows, 1)).reshape(P, -1)
    zero = np.zeros(2 * F, f32)
    parts = {
        "pre_mix": cols(i["norm_pre_mix"]), "post_mix": cols(i["norm_post_mix"]),
        "pre_ffn": cols(i["norm_pre_ffn"]), "post_ffn": cols(i["norm_post_ffn"]),
        "mix": cols(i["mix_norm_2"]), "xattn": cols(i["xattn_norm_2"]), "mem": cols(i["mem_norm_2"]),
        "ffn2": cols(i["ffn_norm_2"]), "final": cols(i["final_norm_2"]),
        "hgrn_gain": cols(i["hgrn_gnorm"]), "gdn_gain": cols(i["gdn_norm_2"]),
        "bounds": cols(i["hgrn_lower_bounds"]), "gdn_conv": taps(list(i["gdn_conv_2"][0])),
        "conv1": taps([*i["ffn_w_conv"][0], zero]),
        "conv2": taps([*i["ffn_conv_2"][0], i["ffn_conv_bias_2"][0]]),
    }
    vecs = np.concatenate([parts[n].astype(f32, copy=False) for n, _ in VEC_PARTS], 1)
    assert vecs.shape[1] == VEC_N
    at = np.arange(P)
    reset = np.ones((P, 2 * T), f32)
    reset[:, ::64] = 0
    ge = (at[:, None] >= at[None, :]).astype(f32)
    neg = np.zeros((P, 384), f32)
    neg[:, 0:P] = neg[:, 2 * P:] = -1e30 * ge
    consts = np.concatenate([np.eye(P, dtype=f32), np.ones((P, P), f32), ge, ge.T, reset, neg], 1)
    masks = np.zeros((P, LEVELS, P), f32)
    for lv in range(LEVELS):
        h = 64 >> lv
        low = (at // h % 2 == 0)
        same = at[:, None] // (2 * h) == at[None, :] // (2 * h)
        masks[:, lv] = same & (low[:, None] != low[None, :])
    gates = np.broadcast_to(np.concatenate([i["gdn_a_log_2"][0], i["gdn_dt_bias_2"][0]]), (P, 16))
    return {
        "xT": tiles(i["x"][0].T), "memT": tiles(i["mem_2"][0].T), "stream": stream,
        "tail": tiles(w_in2[:, 28 * 256:]), "vecs": vecs, "gates": gates, "consts": consts,
        "masks": masks.reshape(P, -1),
    }


def kernel(**inputs):
    import concourse.bacc as bacc
    from concourse.bass_utils import run_bass_kernel_spmd

    arrays = {n: np.ascontiguousarray(a) for n, a in lay_out(
        {n: np.asarray(a) for n, a in inputs.items()}).items()}
    nc = bacc.Bacc("TRN2", target_bir_lowering=False, num_devices=1)
    args = {n: nc.dram_tensor(n, a.shape, mybir.dt.from_np(a.dtype), kind="ExternalInput").ap()
            for n, a in arrays.items()}
    out = nc.dram_tensor("outT", (P, DT, T), F32, kind="ExternalOutput").ap()
    build(nc, **args, outT=out)
    got = run_bass_kernel_spmd(nc, [arrays], core_ids=[0]).results[0]["outT"]
    return np.ascontiguousarray(got.transpose(1, 0, 2).reshape(1, D, T).transpose(0, 2, 1))
```

```python
from contextlib import ExitStack

import numpy as np

import concourse.bass as bass
from concourse import mybir

F32 = mybir.dt.float32
F32R = mybir.dt.float32r
U8 = mybir.dt.uint8
ALU = mybir.AluOpType
ACT = mybir.ActivationFunctionType
AXX = mybir.AxisListType.X

P = 128
T = 256
D = 2048
DT = D // P
F = 5632
FT = F // P
EPS = 1e-6
HEADS = 16
SLOTS = 4
AHEAD = 3
BLK = 4 * 256
LEVELS = 7
F_MIN = 2.0 ** -63

VEC_PARTS = [("pre_mix", DT), ("post_mix", DT), ("pre_ffn", DT), ("post_ffn", DT), ("mix", DT),
             ("xattn", DT), ("mem", DT), ("ffn2", DT), ("final", DT), ("hgrn_gain", 1),
             ("gdn_gain", 1), ("bounds", 2 * HEADS), ("gdn_conv", 24 * 4), ("conv1", 2 * FT * 4),
             ("conv2", 2 * FT * 4)]
VEC_AT, VEC_N = {}, 0
for _name, _n in VEC_PARTS:
    VEC_AT[_name] = VEC_N
    VEC_N += _n

HG_GROUPS, HG_BLOCKS = 5 * 8, 4
UP_GROUPS = 2 * F // 256
DOWN_BLOCKS = F // 512
STREAM = [("hg", HG_GROUPS * 4), ("hgout", 8 * 4), ("up1", UP_GROUPS * 4), ("down1", 8 * DOWN_BLOCKS),
          ("mix", 28 * 4), ("mixout", 8 * 4), ("xq", 2 * 4), ("kv", 4 * 4), ("xo", 8 * 1),
          ("up2", UP_GROUPS * 4), ("down2", 8 * DOWN_BLOCKS)]
GROUPS = {"hg": 40, "hgout": 16, "up1": 44, "down1": 8, "mix": 28, "kv": 4, "mixout": 16, "xq": 2,
          "xo": 8, "up2": 44, "down2": 8}
BLOCK_AT, GROUP_AT, _b, _g = {}, {}, 0, 0
for _name, _n in STREAM:
    BLOCK_AT[_name], GROUP_AT[_name] = _b, _g
    _b += _n
    _g += GROUPS[_name]
N_BLOCKS = _b


class Steps:

    def __init__(self, sem, names):
        self.sem, self.names, self.n = sem, names, len(names)

    def count(self, name, turn=0):
        return self.n * turn + self.names.index(name) + 2

    def before(self, turn):
        return self.n * turn + 1


def drain(steps):
    for _ in steps:
        pass


def pause(n):
    for _ in range(n):
        yield


def slots(n, *sides):
    for _ in range(n):
        for s in sides:
            next(s, None)
        yield


def names(text):
    return text.split()


def build(nc, xT, memT, stream, tail, vecs, gates, consts, masks, outT):
    ctx = ExitStack()
    with ctx:
        def sb(name, shape, dt=F32, stack=None):
            return (stack or ctx).enter_context(nc.sbuf_tensor(name, shape, dt))

        def sem(name):
            return ctx.enter_context(nc.semaphore(name))

        raw = sb("raw", [P, SLOTS, BLK])
        whi = sb("whi", [P, SLOTS, BLK], F32R)
        wlo = sb("wlo", [P, SLOTS, BLK], F32R)
        half = sb("half", [P, 2, 2, T])
        x = sb("x", [P, DT, T])
        vec = sb("vec", [P, VEC_N])
        cst = sb("cst", [P, 4, P])
        msk = sb("msk", [P, LEVELS, P], U8)
        rr = sb("rr", [P, T])
        lnr = sb("lnr", [P, T])
        sqp = sb("sqp", [P, 2, T])
        ident, ones, row_ge, row_le = (cst[:, c, :] for c in range(4))

        with ExitStack() as st:
            hs = sb("hs", [P, DT, 2 * T], F32R, st)
        with ExitStack() as st:
            sb("below_m", [P, DT, T], F32, st)
            m = sb("m", [P, DT, T], F32, st)
        hold = sb("hold", [P, DT, 2 * T])
        with ExitStack() as st:
            sq = sb("sq", [P, DT, T], F32, st)
        with ExitStack() as st:
            os_ = sb("os_", [P, DT, 2 * T], F32R, st)
            hin = sb("hin", [P, 2, 5, 2 * T], F32, st)
            sig = sb("sig", [P, 4, 2 * T], F32, st)
            qk = sb("qk", [P, 3, 2 * T], F32, st)
            lf = sb("lf", [P, 1 + 4 * T], F32, st)
            X = sb("X", [P, 4 * T + 2], F32, st)
            G = sb("G", [P, 2, 4 * T], F32, st)
            LU = sb("LU", [P, 2, 2, 2, P], F32, st)
            AD = sb("AD", [P, 4, P], F32, st)
            AO = sb("AO", [P, 2, 2, P], F32, st)
            vn = sb("vn", [P, 4, P], F32, st)
            tot = sb("tot", [P, 2, 8], F32, st)
            et = sb("et", [P, 2, 8], F32, st)
            reset = sb("reset", [P, 2 * T], F32, st)
            lb = sb("lb", [P, 2, HEADS], F32, st)
            oml = sb("oml", [P, 2, HEADS], F32, st)
        with ExitStack() as st:
            mixs = sb("mixs", [P, DT, 2 * T], F32R, st)
            gin = sb("gin", [P, 2, 4, 2, T + 3], F32, st)
            gts = sb("gts", [P, 2, 16], F32, st)
            gt2 = sb("gt2", [P, 6, 2, 8], F32, st)
            gaw = sb("gaw", [P, 16], F32, st)
            ea = sb("ea", [P, 8], F32, st)
            rrc = sb("rrc", [P, 2], F32, st)
            tl = sb("tl", [P, DT, 16], F32, st)
            tls = sb("tls", [P, 2, DT, 16], F32R, st)
            with ExitStack() as st2:
                sin = sb("sin", [P, 2, 3, 2 * T], F32, st2)
                neg = sb("neg", [P, 384], F32, st2)
                zm = sb("zm", [P, 2, 384], F32, st2)
                se = sb("se", [P, 2, 384], F32, st2)
                sp_ = sb("sp_", [P, 2, 384], F32, st2)
                svn = sb("svn", [P, 4, P], F32, st2)
            with ExitStack() as st2:
                gy = sb("gy", [P, 3, 2 * T], F32, st2)
                gs = sb("gs", [P, 4 * T], F32, st2)
                gr = sb("gr", [P, 4 * T], F32, st2)
                vb = sb("vb", [P, 4, P], F32, st2)
                kbe = sb("kbe", [P, 2, P], F32, st2)
                ktl = sb("ktl", [P, 2, P], F32, st2)
                gbm = sb("gbm", [P, 4, P], F32, st2)
                bbm = sb("bbm", [P, 4, P], F32, st2)
                DTr = sb("DTr", [P, 4, P], F32, st2)
                NLT = sb("NLT", [P, 4, P], F32, st2)
                ATr = sb("ATr", [P, 4, P], F32, st2)
                Tm = sb("Tm", [P, 4, P], F32, st2)
                TT = sb("TT", [P, 4, P], F32, st2)
                Y = sb("Y", [P, 4, P], F32, st2)
                u0 = sb("u0", [P, 2, P], F32, st2)
                Sm = sb("Sm", [P, 2, P], F32, st2)
                nwT = sb("nwT", [P, 2, P], F32, st2)
                vnw = sb("vnw", [P, 2, P], F32, st2)
                qd = sb("qd", [P, 2, P], F32, st2)
        with ExitStack() as st:
            sb("sq_again", [P, DT, T], F32, st)
            xs = sb("xs", [P, 4, 2 * T], F32R, st)
            mems = sb("mems", [P, DT, 2 * T], F32R, st)
            memr = sb("memr", [P, DT, T], F32, st)
            kv = sb("kv", [P, 8, T], F32, st)
            xq = sb("xq", [P, 4, T], F32, st)
        with ExitStack() as st:
            sb("sq_again2", [P, DT, T], F32, st)
            sb("xs_again", [P, 4, 2 * T], F32R, st)
            pr = sb("pr", [P, 8, T], F32, st)
            prT = sb("prT", [P, 4, 2, T], F32, st)
            xvn = sb("xvn", [P, 4, 2, P], F32, st)
            mx = sb("mx", [P, 8], F32, st)
            sm = sb("sm", [P, 8], F32, st)
            rs = sb("rs", [P, 8], F32, st)
        with ExitStack() as st:
            acts = sb("acts", [P, FT, 2 * T], F32R, st)
            cin = sb("cin", [P, 4, T + 2], F32, st)
            cy = sb("cy", [P, 4, T], F32, st)

        acc = ctx.enter_context(nc.psum_tensor("acc", [P, 4, 512], F32))
        ps = ctx.enter_context(nc.psum_tensor("ps", [P, 4, 512], F32))

        raw_in = [sem(f"raw_in{b}") for b in range(SLOTS)]
        hi_ready = sem("hi_ready")
        lo_ready = sem("lo_ready")
        blk_used = sem("blk_used")
        half_out = sem("half_out")
        evac = sem("evac")
        const_in, mem_in, out_done = sem("const_in"), sem("mem_in"), sem("out_done")

        nrm_names = []
        for s, kind in (("n1", "pre"), ("n2", "post"), ("n3", "pre"), ("n4", "post"), ("n5", "pre"),
                        ("n8", "onto"), ("n7", "memory"), ("n10", "onto"), ("n12", "final")):
            nrm_names.append((s, kind))
        nA, nV, nP = [], [], []
        for s, kind in nrm_names:
            root = [f"{s}_ln", f"{s}_r"]
            if kind == "pre":
                nA += [f"{s}_{w}{c}" for w in ("sq", "hi") for c in range(4)] + root
                nP += [f"{s}_ssq"]
                nV += [f"{s}_lo{c}" for c in range(4)]
            elif kind == "memory":
                nA += [f"{s}_sq{c}" for c in range(4)] + root + [f"{s}_hi{c}" for c in range(4)]
                nP += [f"{s}_ssq"]
                nV += [f"{s}_{w}" for w in ("h0", "h1", "lo0", "h2", "lo1", "h3", "lo2", "lo3")]
            else:
                nP += [f"{s}_ss{g}" for g in range(8)]
                nA += [f"{s}_{w}{g}" for g in range(8) for w in (("sq", "hi") if kind == "onto" else ("sq",))]
                nA += root
                if kind == "onto":
                    nV += [f"{s}_lo{g}" for g in range(8)]
                elif kind == "post":
                    nV += [f"{s}_{w}{c}" for c in range(4) for w in ("t", "x")]
                else:
                    nV += [f"{s}_h{c}" for c in range(4)]
        norm_act = Steps(sem("norm_act"), nA)
        norm_vec = Steps(sem("norm_vec"), nV)
        norm_pe = Steps(sem("norm_pe"), nP)
        hg_act = Steps(sem("hg_act"), names("ex et er vn e1 ad ao e2 e3 e4 e5 e6"))
        hg_act_in = Steps(sem("hg_act_in"), names("sig ln"))
        hg_vec_in = Steps(sem("hg_vec_in"), names("g f clamp"))
        hg_act_out = Steps(sem("hg_act_out"), names("osq oln or"))
        hg_vec = Steps(sem("hg_vec"), names(
            "q k bf bb totf totb er g64l g64u lu1 lu0 ks d1l d1u p1l p1u c0 "
            "d2l d2u p2l p2u c1 d3l d3u p3l p3u c2 d4l d4u p4l p4u c3 "
            "d5l d5u p5l p5u c4 d6l d6u p6l p6u c5 c6"))
        hg_vec_out = Steps(sem("hg_vec_out"), names("og os hi lo"))
        hg_pe = Steps(sem("hg_pe"), names("vt diag l128 g0 g1 g2 g3 g4 g5 g6"))
        hg_pe_out = Steps(sem("hg_pe_out"), names("pv ssq"))
        summed = sem("summed")
        copies_begun = sem("copies_begun")
        gate_in, neg_in, gpad_set, mem_out = sem("gate_in"), sem("neg_in"), sem("gpad_set"), sem("mem_out")
        gt_act = Steps(sem("gt_act"), names("tlh ea beta abs e l egc egt"))
        gt_vec = Steps(sem("gt_vec"), names("tll rr a sp g cum tot bgc"))
        gt_pe = Steps(sem("gt_pe"), names("lg cum"))
        sb_act = Steps(sem("sb_act"), names("vn abs e l w hi"))
        sb_vec = Steps(sem("sb_vec"), names("zm sp w lo"))
        sb_pe = Steps(sem("sb_pe"), names("z cs o"))
        gd_act = Steps(sem("gd_act"), names(
            "silu sqk ln r qe dt vb kbe ktl y0 y1 y2 y3 y4 y5 y6 u0 nw"))
        gd_act_out = Steps(sem("gd_act_out"), names("vn osq oln or"))
        gd_vec = Steps(sem("gd_vec"), names(
            "c0 c1 c2 c3 gbm bbm q k d nl0 at0 nl at qd Tm TT "
            "t0 tt0 t1 tt1 t2 tt2 t3 tt3 t4 tt4 t5 tt5 t6 tt6 S"))
        gd_vec_out = Steps(sem("gd_vec_out"), names("og os hi lo"))
        gd_pe = Steps(sem("gd_pe"), names(
            "ssq rows kk tr y0 z0 y1 z1 y2 z2 y3 z3 y4 z4 y5 z5 y6 z6 uw S"))
        gd_pe_out = Steps(sem("gd_pe_out"), names("vn o os"))
        xa_act = Steps(sem("xa_act"), names("p vn pt hi"))
        xa_vec = Steps(sem("xa_vec"), names("mx nmx rs p lo"))
        xa_pe = Steps(sem("xa_pe"), names("z vt pt o"))
        hg_exp = sem("hg_exp")
        hg_set = sem("hg_set")
        mlp_vec = [Steps(sem(f"mlp_vec{k}"), names(
            "a00 a01 a10 a11 a20 a21 b00 b01 b10 b11 b20 b21 mul hi lo")) for k in range(2)]
        mlp_act = [Steps(sem(f"mlp_act{k}"), names("silu")) for k in range(2)]
        pad_set = [sem(f"pad_set{k}") for k in range(2)]

        def at(lap, k):
            return lap + k // SLOTS, k % SLOTS

        def round_hi(act, lap, k):
            r, b = at(lap, k)
            act.wait_ge(raw_in[b], 16 * r + 16)
            act.wait_ge(blk_used, SLOTS * r + b + 1)
            nc.scalar.activation(whi[:, b, :], raw[:, b, :], ACT.Copy).then_inc(hi_ready, 1)

        def take_lo(dve, lap, k):
            r, b = at(lap, k)
            dve.wait_ge(hi_ready, SLOTS * r + b + 1)
            nc.vector.tensor_tensor(wlo[:, b, :], raw[:, b, :], whi[:, b, :].bitcast(F32),
                                    ALU.subtract).then_inc(lo_ready, 1)

        def copy_half(act, lap, k, group, par):
            r, b = at(lap, k)
            act.wait_ge(blk_used, SLOTS * r + b + 1 + SLOTS)
            act.wait_ge(evac, group + 1)
            nc.scalar.activation(half[:, par], acc[:, 2 * par:2 * par + 2, T:2 * T],
                                 ACT.Copy).then_inc(half_out, 1)

        def evacuate(dve, dest, group, par):
            dve.wait_ge(half_out, group + 1)
            nc.vector.tensor_tensor(dest, acc[:, 2 * par:2 * par + 2, 0:T], half[:, par],
                                    ALU.add).then_inc(evac, 1)

        def sum_halves(dve, group, par, plain):
            dve.wait_ge(half_out, group + 1)
            nc.vector.tensor_tensor(half[:, par], acc[:, 2 * par:2 * par + 2, 0:T], half[:, par],
                                    ALU.add).then_inc(summed, 1)
            dve.wait_ge(summed, group - plain + 1)

        def evacuate_scaled(dve, dest, group, par, plain, norm):
            sum_halves(dve, group, par, plain)
            dve.wait_ge(norm_act.sem, norm_act.count(f"{norm}_r"))
            nc.vector.tensor_tensor(dest, half[:, par], rr[:].unsqueeze(1).broadcast_to([P, 2, T]),
                                    ALU.mult).then_inc(evac, 1)

        def evacuate_onto(dve, dest, group, par, plain):
            sum_halves(dve, group, par, plain)
            dve.wait_ge(evac, group + 1)
            nc.vector.tensor_tensor(dest, dest, half[:, par], ALU.add).then_inc(evac, 1)

        def multiply(pe, lap, k, group, par, src, kb, first, last, side=None, norm=None):
            r, b = at(lap, k)
            if kb == first:
                pe.wait_ge(evac, group + 1)
            if norm in ("up1", "up2"):
                if kb == DOWN_BLOCKS - 1:
                    pe.wait_ge(mlp_vec[norm == "up2"].sem, mlp_vec[norm == "up2"].count("lo", UP_GROUPS // 2 - 1))
                elif kb == 0:
                    pe.wait_ge(mlp_vec[norm == "up2"].sem, mlp_vec[norm == "up2"].count("lo", UP_GROUPS // 2 - 2))
            elif norm in ("n8", "n10"):
                pe.wait_ge(norm_vec.sem, norm_vec.count(f"{norm}_lo{2 * kb + 1}"))
            elif norm is not None:
                pe.wait_ge(norm_vec.sem, norm_vec.count(f"{norm}_lo{kb}"))
            pe.wait_ge(lo_ready, SLOTS * r + b + 1 + SLOTS)
            for n in range(2):
                for q in range(4):
                    c, kt = q * 256 + n * P, 4 * kb + q
                    nc.tensor.matmul(acc[:, 2 * par + n, :], whi[:, b, c:c + P], src[:, kt, :],
                                     start=(kt == 4 * first), stop=False)
                    mm = nc.tensor.matmul(acc[:, 2 * par + n, 0:T], wlo[:, b, c:c + P],
                                          src[:, kt, 0:T], start=False, stop=(kt == 4 * last + 3))
                if n == 1:
                    mm.then_inc(blk_used, 1)
                if side is not None:
                    next(side, None)

        def root(act, s):
            nc.scalar.activation(lnr[:], ps[:, 0, 0:T], ACT.Ln, bias=EPS,
                                               scale=1.0 / D).then_inc(norm_act.sem, 1)
            act.wait_ge(norm_act.sem, norm_act.count(f"{s}_ln"))
            nc.scalar.activation(rr[:], lnr[:], ACT.Exp, scale=-0.5).then_inc(norm_act.sem, 1)

        def pre_scalar(act, s, gain, ready):
            for c in range(4):
                ready(act, c)
                nc.scalar.activation(sq[:, 4 * c:4 * c + 4, :],
                                                   x[:, 4 * c:4 * c + 4, :], ACT.Square).then_inc(norm_act.sem, 1)
            for c in range(4):
                for t in range(4 * c, 4 * c + 4):
                    g = VEC_AT[gain] + t
                    ins = nc.scalar.activation(hs[:, t, 0:T], x[:, t, :], ACT.Copy, scale=vec[:, g:g + 1])
                ins.then_inc(norm_act.sem, 1)
            act.wait_ge(norm_pe.sem, norm_pe.count(f"{s}_ssq"))
            root(act, s)

        def pre_tensor(pe, s):
            for t in range(DT):
                if t % 4 == 0:
                    pe.wait_ge(norm_act.sem, norm_act.count(f"{s}_sq{t // 4}"))
                mm = nc.tensor.matmul(ps[:, 0, 0:T], ones, sq[:, t, :], start=(t == 0), stop=(t == DT - 1))
            mm.then_inc(norm_pe.sem, 1)

        def low_part(t, gain):
            g = VEC_AT[gain] + t
            return nc.vector.scalar_tensor_tensor(hs[:, t, T:2 * T], x[:, t, :], vec[:, g:g + 1],
                                                  hs[:, t, 0:T].bitcast(F32), ALU.mult, ALU.subtract)

        def pre_vector(dve, s, gain):
            for c in range(4):
                dve.wait_ge(norm_act.sem, norm_act.count(f"{s}_hi{c}"))
                for t in range(4 * c, 4 * c + 4):
                    ins = low_part(t, gain)
                ins.then_inc(norm_vec.sem, 1)

        def follow_scalar(act, s, src, group, g, gain=None):
            act.wait_ge(evac, group + 3)
            if g:
                act.wait_ge(norm_pe.sem, norm_pe.count(f"{s}_ss{g - 1}"))
            nc.scalar.activation(sqp[:], src[:, 2 * g:2 * g + 2, :], ACT.Square).then_inc(norm_act.sem, 1)
            if gain is not None:
                for t in range(2 * g, 2 * g + 2):
                    c = VEC_AT[gain] + t
                    ins = nc.scalar.activation(hs[:, t, 0:T], x[:, t, :], ACT.Copy, scale=vec[:, c:c + 1])
                ins.then_inc(norm_act.sem, 1)

        def follow_tensor(pe, s, g):
            pe.wait_ge(norm_act.sem, norm_act.count(f"{s}_sq{g}"))
            for t in range(2):
                mm = nc.tensor.matmul(ps[:, 0, 0:T], ones, sqp[:, t, :], start=(g == 0 and t == 0),
                                      stop=(g == 7 and t == 1))
            mm.then_inc(norm_pe.sem, 1)

        def follow_vector(dve, s, g, gain):
            dve.wait_ge(norm_act.sem, norm_act.count(f"{s}_hi{g}"))
            for t in range(2 * g, 2 * g + 2):
                ins = low_part(t, gain)
            ins.then_inc(norm_vec.sem, 1)

        def follow(eng, what, s, src, first, grp, gain):
            if what == "act" and 1 <= grp <= 8:
                follow_scalar(eng, s, src, first + grp - 1, grp - 1, gain)
            if what == "pe" and grp >= 2:
                follow_tensor(eng, s, grp - 2)
            if what == "dve" and grp >= 2 and gain is not None:
                follow_vector(eng, s, grp - 2, gain)
            if what == "act" and grp == 9:
                eng.wait_ge(norm_pe.sem, norm_pe.count(f"{s}_ss7"))
                root(eng, s)

        def memory_scalar(act):
            yield
            act.wait_ge(mem_in, 16)
            for c in range(4):
                nc.scalar.activation(sq[:, 4 * c:4 * c + 4, :], memr[:, 4 * c:4 * c + 4, :],
                                                   ACT.Square).then_inc(norm_act.sem, 1)
                if c == 1:
                    yield
            yield
            act.wait_ge(norm_pe.sem, norm_pe.count("n7_ssq"))
            nc.scalar.activation(lnr[:], ps[:, 0, 0:T], ACT.Ln, bias=EPS,
                                               scale=1.0 / D).then_inc(norm_act.sem, 1)
            act.wait_ge(norm_act.sem, norm_act.count("n7_ln"))
            nc.scalar.activation(lnr[:], lnr[:], ACT.Exp, scale=-0.5).then_inc(norm_act.sem, 1)
            yield
            for c in range(4):
                act.wait_ge(norm_vec.sem, norm_vec.count(f"n7_h{c}"))
                nc.scalar.activation(mems[:, 4 * c:4 * c + 4, 0:T],
                                                   sq[:, 4 * c:4 * c + 4, :], ACT.Copy).then_inc(norm_act.sem, 1)
                yield

        def memory_tensor(pe):
            yield from pause(5)
            for c in range(4):
                pe.wait_ge(norm_act.sem, norm_act.count(f"n7_sq{c}"))
                for t in range(4 * c, 4 * c + 4):
                    mm = nc.tensor.matmul(ps[:, 0, 0:T], ones, sq[:, t, :], start=(t == 0),
                                          stop=(t == DT - 1))
            mm.then_inc(norm_pe.sem, 1)

        def memory_vector(dve):
            yield from pause(3)
            dve.wait_ge(norm_act.sem, norm_act.count("n7_r"))
            for c in range(5):
                if c < 4:
                    for t in range(4 * c, 4 * c + 4):
                        g = VEC_AT["mem"] + t
                        ins = nc.vector.scalar_tensor_tensor(sq[:, t, :], memr[:, t, :], vec[:, g:g + 1],
                                                             lnr[:], ALU.mult, ALU.mult)
                    ins.then_inc(norm_vec.sem, 1)
                if c:
                    dve.wait_ge(norm_act.sem, norm_act.count(f"n7_hi{c - 1}"))
                    nc.vector.tensor_tensor(
                        mems[:, 4 * c - 4:4 * c, T:2 * T], sq[:, 4 * c - 4:4 * c, :],
                        mems[:, 4 * c - 4:4 * c, 0:T].bitcast(F32), ALU.subtract).then_inc(norm_vec.sem, 1)
                yield

        def norm_post_vector(dve, s, gain):
            dve.wait_ge(norm_act.sem, norm_act.count(f"{s}_r"))
            for c in range(4):
                for t in range(4 * c, 4 * c + 4):
                    g = VEC_AT[gain] + t
                    ins = nc.vector.scalar_tensor_tensor(m[:, t, :], m[:, t, :], vec[:, g:g + 1],
                                                         rr[:], ALU.mult, ALU.mult)
                ins.then_inc(norm_vec.sem, 1)
                dve.wait_ge(norm_vec.sem, norm_vec.count(f"{s}_t{c}"))
                nc.vector.tensor_tensor(x[:, 4 * c:4 * c + 4, :], x[:, 4 * c:4 * c + 4, :],
                                                      m[:, 4 * c:4 * c + 4, :], ALU.add).then_inc(norm_vec.sem, 1)

        def final_vector(dve, s, gain):
            dve.wait_ge(norm_act.sem, norm_act.count(f"{s}_r"))
            dve.wait_ge(evac, GROUP_AT["down2"] + 7 + 3)
            for c in range(4):
                for t in range(4 * c, 4 * c + 4):
                    g = VEC_AT[gain] + t
                    ins = nc.vector.scalar_tensor_tensor(sq[:, t, :], x[:, t, :], vec[:, g:g + 1],
                                                         rr[:], ALU.mult, ALU.mult)
                ins.then_inc(norm_vec.sem, 1)

        def product(eng, what, name, kbs, loops, per_loop, src=None, last=False, dest=m, side=None,
                    norm=None, plain=0, onto=False, then=None, gain=None):
            lap0, g0 = BLOCK_AT[name] // SLOTS, GROUP_AT[name]
            laps = per_loop * kbs // SLOTS

            def body(i, final):
                lap, g = lap0 + laps * i, g0 + per_loop * i
                for k in range(per_loop * kbs):
                    grp, kb = divmod(k, kbs)
                    ahead = not (final and k + AHEAD >= per_loop * kbs)
                    if what == "act":
                        if ahead:
                            round_hi(eng, lap, k + AHEAD)
                        if side is not None:
                            next(side, None)
                        if kb == kbs - 1:
                            copy_half(eng, lap, k, g + grp, grp % 2)
                    elif what == "dve":
                        if ahead:
                            take_lo(eng, lap, k + AHEAD)
                        if side is not None:
                            next(side, None)
                        if kb == kbs - 1:
                            to = dest[:, bass.ds((per_loop * i + grp) * 2, 2), :]
                            if onto:
                                evacuate_onto(eng, to, g + grp, grp % 2, plain)
                            elif name == "xq":
                                evacuate_scaled(eng, to, g + grp, grp % 2, plain, "n8")
                            else:
                                evacuate(eng, to, g + grp, grp % 2)
                    else:
                        multiply(eng, lap, k, g + grp, grp % 2, src, kb, 0, kbs - 1, side, norm)
                    if then and kb == kbs - 1:
                        follow(eng, what, then, dest, g0, per_loop * i + grp, gain)

            if then or loops == 1:
                for i in range(loops):
                    body(i, last and i == loops - 1)
                if then:
                    for grp in (8, 9):
                        follow(eng, what, then, dest, g0, grp, gain)
            else:
                with eng.Fori(0, loops) as i:
                    body(i, False)

        def split_product(eng, what, name, src, side, dest, plain, then, gain=None):
            lap, g = BLOCK_AT[name] // SLOTS, GROUP_AT[name]
            for k in range(24):
                grp, kb = divmod(k, 3)
                if what == "act":
                    round_hi(eng, lap, k + AHEAD)
                    next(side, None)
                    if kb == 2:
                        copy_half(eng, lap, k, g + grp, grp % 2)
                elif what == "dve":
                    take_lo(eng, lap, k + AHEAD)
                    next(side, None)
                    if kb == 2 and name == "hgout":
                        evacuate(eng, m[:, 2 * grp:2 * grp + 2, :], g + grp, grp % 2)
                    elif kb == 2:
                        evacuate_onto(eng, x[:, 2 * grp:2 * grp + 2, :], g + grp, grp % 2, plain)
                else:
                    multiply(eng, lap, k, g + grp, grp % 2, src, kb, 0, 2, side)
            drain(side)
            if what == "pe":
                if name == "hgout":
                    eng.wait_ge(hg_vec_out.sem, hg_vec_out.count("lo", 7))
                else:
                    eng.wait_ge(gd_vec_out.sem, gd_vec_out.count("lo", 3))
            for grp in range(8):
                k, ga, par = 24 + grp, g + 8 + grp, grp % 2
                if what == "act":
                    round_hi(eng, lap, k + AHEAD)
                    copy_half(eng, lap, k, ga, par)
                elif what == "dve":
                    take_lo(eng, lap, k + AHEAD)
                    evacuate_onto(eng, dest[:, 2 * grp:2 * grp + 2, :], ga, par, plain)
                else:
                    multiply(eng, lap, k, ga, par, src, 3, 3, 3)
                follow(eng, what, then, dest, g + 8, grp, gain)
            for grp in (8, 9):
                follow(eng, what, then, dest, g + 8, grp, gain)

        def halves(ap, h):
            return ap.rearrange("p d (n u h) -> p d n u h", u=2, h=h)

        def Xd():
            return X[:, 0:4 * T].rearrange("p (d n) -> p d n", d=2)

        def middle(h):
            v = X[:, :].rearrange("p (d n) -> p d n", d=2)
            return v[:, :, h - 1:2 * T:2 * h].unsqueeze(3).broadcast_to([P, 2, T // h, h])

        EXv = sig[:, 0:2, :]
        ERv = sig[:, 2:4, :]
        LOWER, UPPER = qk[:, 0:2, :], qk[:, 1:3, :]

        def hg_vector_in(dve, turn, par):
            n = hin[:, par]
            yield from pause(18)
            dve.wait_ge(hg_act_in.sem, hg_act_in.count("sig", turn))
            nc.vector.tensor_tensor(n[:, 3], n[:, 3], sig[:, 3], ALU.mult).then_inc(hg_vec_in.sem, 1)
            for d in range(2):
                for h in range(2):
                    ins = nc.vector.tensor_scalar(
                        sig[:, d, h * T:(h + 1) * T], sig[:, d, h * T:(h + 1) * T],
                        oml[:, d, bass.ds(2 * turn + h, 1)], lb[:, d, bass.ds(2 * turn + h, 1)],
                        ALU.mult, ALU.add)
            ins.then_inc(hg_vec_in.sem, 1)
            dve.wait_ge(hg_vec_in.sem, hg_vec_in.count("f", turn))
            nc.vector.tensor_scalar(
                lf[:, 1:1 + 4 * T], sig[:, 0:2, :].rearrange("p d n -> p (d n)"), F_MIN, None,
                ALU.max).then_inc(hg_vec_in.sem, 1)

        def hg_vector(dve, turn, par):
            n = hin[:, par]
            dve.wait_ge(hg_pe.sem, hg_pe.before(turn))
            nc.vector.tensor_tensor(qk[:, 1], n[:, 2], sig[:, 2], ALU.mult).then_inc(hg_vec.sem, 1)
            nc.vector.tensor_scalar(qk[:, 0:3:2, :], sig[:, 0:2, :], -1.0, 1.0, ALU.mult,
                                                ALU.add).then_inc(hg_vec.sem, 1)
            dve.wait_ge(hg_act_in.sem, hg_act_in.count("ln", turn))
            nc.vector.tensor_tensor_scan(X[:, 0:2 * T], reset[:], lf[:, 1:1 + 2 * T], 0.0,
                                                     ALU.mult, ALU.add).then_inc(hg_vec.sem, 1)
            nc.vector.tensor_tensor_scan(X[:, 2 * T:4 * T], lf[:, 2 * T:4 * T], reset[:], 0.0,
                                                     ALU.add, ALU.mult).then_inc(hg_vec.sem, 1)
            yield
            dve.wait_ge(hg_vec.sem, hg_vec.count("bb", turn))
            last = X[:, 0:4 * T].rearrange("p (d c n) -> p d c n", d=2, n=64)[:, :, :, 63]
            lastf = lf[:, 1:1 + 4 * T].rearrange("p (d c n) -> p d c n", d=2, n=64)[:, 1, :, 63]
            nc.vector.tensor_copy(tot[:, 0, :], last[:, 0, :]).then_inc(hg_vec.sem, 1)
            nc.vector.tensor_tensor(tot[:, 1, :], last[:, 1, :], lastf, ALU.add).then_inc(hg_vec.sem, 1)
            dve.wait_ge(hg_vec.sem, hg_vec.count("totb", turn))
            nc.vector.tensor_tensor(
                G[:, 0].rearrange("p (c n) -> p c n", n=64),
                tot[:].rearrange("p d c -> p (d c)").unsqueeze(2).broadcast_to([P, 16, 64]),
                X[:, 0:4 * T].rearrange("p (c n) -> p c n", n=64), ALU.subtract).then_inc(hg_vec.sem, 1)
            yield from pause(3)
            dve.wait_ge(hg_act.sem, hg_act.count("er", turn))
            g = halves(G[:, 0].rearrange("p (d n) -> p d n", d=2), 64)
            lo_, up_ = halves(LOWER, 64), halves(UPPER, 64)
            ex_, er_ = halves(EXv, 64), halves(ERv, 64)
            nc.vector.tensor_tensor(g[:, :, :, 0, :], lo_[:, :, :, 0, :], er_[:, :, :, 0, :],
                                                ALU.mult).then_inc(hg_vec.sem, 1)
            nc.vector.tensor_tensor(g[:, :, :, 1, :], up_[:, :, :, 1, :], ex_[:, :, :, 1, :],
                                                ALU.mult).then_inc(hg_vec.sem, 1)
            yield

            def chunk(ap, c):
                return ap.rearrange("p d (h c n) -> p d h c n", h=2, n=64)[:, :, :, c, :]

            def whole(c):
                return et[:, :, c:8:4].unsqueeze(3).broadcast_to([P, 2, 2, 64])

            nc.vector.tensor_tensor(LU[:, 0, :, :, 64:128], chunk(LOWER, 1), chunk(ERv, 1), ALU.mult)
            nc.vector.tensor_tensor(LU[:, 1, :, :, 0:64], chunk(UPPER, 2), chunk(EXv, 2),
                                                ALU.mult).then_inc(hg_vec.sem, 1)
            dve.wait_ge(hg_vec.sem, hg_vec.count("g64u", turn))
            G0 = G[:, 0].rearrange("p (d n) -> p d n", d=2)
            nc.vector.tensor_tensor(LU[:, 0, :, :, 0:64], chunk(G0, 0), whole(1), ALU.mult)
            nc.vector.tensor_tensor(LU[:, 1, :, :, 64:128], chunk(G0, 3), whole(2),
                                                ALU.mult).then_inc(hg_vec.sem, 1)
            nc.vector.tensor_tensor(n[:, 2], qk[:, 0], qk[:, 2], ALU.add).then_inc(hg_vec.sem, 1)
            yield
            for lv in range(1, LEVELS):
                h = 64 >> lv
                s = lv % 2
                gl = G[:, s].rearrange("p (d n) -> p d n", d=2)
                if lv >= 2:
                    dve.wait_ge(hg_pe.sem, hg_pe.count(f"g{lv - 2}", turn))
                nc_low, nc_up = halves(gl, h)[:, :, :, 0, :], halves(gl, h)[:, :, :, 1, :]
                nc.vector.tensor_tensor(nc_low, middle(h), halves(Xd(), h)[:, :, :, 0, :],
                                                    ALU.subtract).then_inc(hg_vec.sem, 1)
                nc.vector.tensor_tensor(nc_up, halves(Xd(), h)[:, :, :, 1, :], middle(h),
                                                    ALU.subtract).then_inc(hg_vec.sem, 1)
                yield
                dve.wait_ge(hg_act.sem, hg_act.count(f"e{lv}", turn))
                nc.vector.tensor_tensor(nc_low, nc_low, halves(LOWER, h)[:, :, :, 0, :],
                                                    ALU.mult).then_inc(hg_vec.sem, 1)
                nc.vector.tensor_tensor(nc_up, nc_up, halves(UPPER, h)[:, :, :, 1, :],
                                                    ALU.mult).then_inc(hg_vec.sem, 1)
                merge(dve, turn, lv - 1)
                yield
            yield
            merge(dve, turn, LEVELS - 1)

        out_sq, out_rms = G[:, 1, 0:2 * T], G[:, 1, 2 * T:4 * T]

        def hg_vector_out(dve, turn, par):
            n = hin[:, par]
            yield from pause(3)
            dve.wait_ge(hg_act_out.sem, hg_act_out.count("or", turn))
            og = out_sq
            gain = vec[:, VEC_AT["hgrn_gain"]:VEC_AT["hgrn_gain"] + 1]
            nc.vector.scalar_tensor_tensor(og, ps[:, 0, :], gain, out_rms, ALU.mult, ALU.mult).then_inc(hg_vec_out.sem, 1)
            dve.wait_ge(hg_vec_out.sem, hg_vec_out.count("og", turn))
            nc.vector.tensor_tensor(og, og, n[:, 3], ALU.mult).then_inc(hg_vec_out.sem, 1)
            dve.wait_ge(hg_vec_out.sem, hg_vec_out.count("os", turn))
            o2 = og.rearrange("p (h t) -> p h t", h=2)
            dst = os_[:, bass.ds(2 * turn, 2), :]
            nc.vector.tensor_scalar(dst[:, :, 0:T], o2, 1.0, None, ALU.mult).then_inc(hg_vec_out.sem, 1)
            dve.wait_ge(hg_vec_out.sem, hg_vec_out.count("hi", turn))
            nc.vector.tensor_tensor(dst[:, :, T:2 * T], o2, dst[:, :, 0:T].bitcast(F32),
                                                ALU.subtract).then_inc(hg_vec_out.sem, 1)

        def merge(dve, turn, lv):
            dve.wait_ge(hg_pe.sem, hg_pe.count(f"g{lv}", turn))
            if lv == 0:
                dve.wait_ge(hg_act.sem, hg_act.count("ad", turn))
            else:
                dve.wait_ge(hg_vec.sem, hg_vec.count(f"c{lv - 1}", turn))
            dve.sem_inc(copies_begun, 1)
            nc.vector.copy_predicated(
                AD[:], msk[:, lv, :].unsqueeze(1).broadcast_to([P, 4, P]),
                ps[:, 2 + lv % 2, :].rearrange("p (a b) -> p a b", a=4)).then_inc(hg_vec.sem, 1)

        def hg_scalar_in(act, turn, par):
            yield from pause(16)
            act.wait_ge(evac, GROUP_AT["hg"] + 5 * turn + 3 + 3)
            nc.scalar.activation(sig[:], hin[:, par, 0:4], ACT.Sigmoid).then_inc(hg_act_in.sem, 1)
            yield from pause(3)
            act.wait_ge(hg_vec_in.sem, hg_vec_in.count("clamp", turn))
            nc.scalar.activation(lf[:, 1:1 + 4 * T], lf[:, 1:1 + 4 * T], ACT.Ln).then_inc(hg_act_in.sem, 1)

        def hg_scalar(act, turn, par):
            yield
            act.wait_ge(hg_vec.sem, hg_vec.count("bb", turn))
            nc.scalar.activation(EXv, Xd(), ACT.Exp).then_inc(hg_act.sem, 1)
            yield
            act.wait_ge(hg_vec.sem, hg_vec.count("er", turn))
            nc.scalar.activation(et[:], tot[:], ACT.Exp).then_inc(hg_act.sem, 1)
            nc.scalar.activation(ERv, G[:, 0].rearrange("p (d n) -> p d n", d=2), ACT.Exp).then_inc(hg_act.sem, 1)
            yield
            act.wait_ge(hg_pe.sem, hg_pe.count("vt", turn))
            nc.scalar.activation(vn[:].rearrange("p a b -> p (a b)"), ps[:, 1, :], ACT.Copy).then_inc(hg_act.sem, 1)
            yield from pause(4)
            act.wait_ge(hg_vec.sem, hg_vec.count("d1u", turn))
            nc.scalar.activation(G[:, 1], G[:, 1], ACT.Exp).then_inc(hg_act.sem, 1)
            act.wait_ge(hg_pe.sem, hg_pe.count("diag", turn))
            nc.scalar.activation(AD[:].rearrange("p a b -> p (a b)"), ps[:, 1, :], ACT.Copy).then_inc(hg_act.sem, 1)
            act.wait_ge(hg_pe.sem, hg_pe.count("l128", turn))
            nc.scalar.activation(AO[:].rearrange("p d h b -> p (d h b)"), ps[:, 0, :], ACT.Copy).then_inc(hg_act.sem, 1)
            for lv in range(2, LEVELS):
                yield from pause(2)
                act.wait_ge(hg_vec.sem, hg_vec.count(f"d{lv}u", turn))
                nc.scalar.activation(G[:, lv % 2], G[:, lv % 2], ACT.Exp).then_inc(hg_act.sem, 1)

        def hg_scalar_out(act, turn, par):
            yield
            act.wait_ge(hg_pe_out.sem, hg_pe_out.count("pv", turn))
            nc.scalar.activation(out_sq, ps[:, 0, :], ACT.Square).then_inc(hg_act_out.sem, 1)
            yield
            act.wait_ge(hg_pe_out.sem, hg_pe_out.count("ssq", turn))
            nc.scalar.activation(out_rms, ps[:, 2, :], ACT.Ln, bias=EPS, scale=1.0 / P).then_inc(hg_act_out.sem, 1)
            act.wait_ge(hg_act_out.sem, hg_act_out.count("oln", turn))
            nc.scalar.activation(out_rms, out_rms, ACT.Exp, scale=-0.5).then_inc(hg_act_out.sem, 1)

        def hg_tensor(pe, turn, par):
            n = hin[:, par]
            yield from pause(3)
            pe.wait_ge(hg_vec.sem, hg_vec.before(turn))
            pe.wait_ge(evac, GROUP_AT["hg"] + 5 * turn + 4 + 3)
            for a in range(4):
                mm = nc.tensor.transpose(ps[:, 1, a * P:(a + 1) * P], n[:, 4, a * P:(a + 1) * P], ident)
            mm.then_inc(hg_pe.sem, 1)
            yield from pause(10)
            pe.wait_ge(hg_act.sem, hg_act.count("vn", turn))
            pe.wait_ge(hg_vec.sem, hg_vec.count("ks", turn))
            for a in range(4):
                mm = nc.tensor.matmul(ps[:, 1, a * P:(a + 1) * P], n[:, 2, a * P:(a + 1) * P],
                                      qk[:, 1, a * P:(a + 1) * P], start=True, stop=True)
            mm.then_inc(hg_pe.sem, 1)
            for d in range(2):
                for h in range(2):
                    mm = nc.tensor.matmul(ps[:, 0, (2 * d + h) * P:(2 * d + h + 1) * P], LU[:, d, d, h, :],
                                          LU[:, 1 - d, d, h, :], start=True, stop=True)
            mm.then_inc(hg_pe.sem, 1)
            yield
            for lv in range(LEVELS):
                if lv == 0:
                    pe.wait_ge(hg_vec.sem, hg_vec.count("ks", turn))
                else:
                    pe.wait_ge(hg_vec.sem, hg_vec.count(f"p{lv}u", turn))
                if lv >= 2:
                    pe.wait_ge(hg_vec.sem, hg_vec.count(f"c{lv - 2}", turn))
                for d in range(2):
                    for a in range(4):
                        g = G[:, lv % 2, (4 * d + a) * P:(4 * d + a + 1) * P]
                        o = ps[:, 2 + lv % 2, a * P:(a + 1) * P]
                        mm = nc.tensor.matmul(half_of(o, lv, 1 - d), g, half_of(g, lv, 1 - d),
                                              start=True, stop=True)
                mm.then_inc(hg_pe.sem, 1)
                yield from pause(4 if lv else 3)

        def half_of(ap, lv, u):
            return ap.rearrange("p (n u h) -> p n u h", u=2, h=64 >> lv)[:, :, u, :]

        def hg_tensor_out(pe, turn, par):
            yield
            pe.wait_ge(hg_vec.sem, hg_vec.count("c6", turn))
            pe.wait_ge(hg_act.sem, hg_act.count("ao", turn))
            for h in range(2):
                for t in range(2):
                    o = ps[:, 0, (2 * h + t) * P:(2 * h + t + 1) * P]
                    nc.tensor.matmul(o, vn[:, 2 * h + t, :], AD[:, 2 * h + t, :], start=True, stop=False)
                    mm = nc.tensor.matmul(o, vn[:, 2 * h + 1 - t, :], AO[:, 1 - t, h, :], start=False,
                                          stop=True)
            mm.then_inc(hg_pe_out.sem, 1)
            yield from pause(2)
            pe.wait_ge(hg_act_out.sem, hg_act_out.count("osq", turn))
            nc.tensor.matmul(ps[:, 2, :], ones, out_sq, start=True, stop=True).then_inc(hg_pe_out.sem, 1)

        def hg_stage(eng, what, turn_expr, par, side, norm=False):
            lap, g = BLOCK_AT["hg"] // SLOTS + 5 * turn_expr, GROUP_AT["hg"] + 5 * turn_expr
            for k in range(20):
                grp, kb = divmod(k, 4)
                gp = (par + grp) % 2
                if what == "act":
                    round_hi(eng, lap, k + AHEAD)
                    next(side, None)
                    if kb == 3:
                        copy_half(eng, lap, k, g + grp, gp)
                elif what == "dve":
                    take_lo(eng, lap, k + AHEAD)
                    next(side, None)
                    if kb == 3:
                        evacuate_scaled(eng, hin[:, par, grp].rearrange("p (h t) -> p h t", h=2),
                                        g + grp, gp, 0, "n1")
                else:
                    multiply(eng, lap, k, g + grp, gp, hs, kb, 0, 3, side,
                             "n1" if par == 0 and norm and k < 4 else None)
            drain(side)

        def hg_all(eng, what, take_in, attend, put_out):
            n = 2 if what == "pe" else 1
            hg_stage(eng, what, 0, 0, slots(20 * n, take_in(eng, 0, 0)), norm=True)
            hg_stage(eng, what, 1, 1, slots(20 * n, attend(eng, 0, 0), take_in(eng, 1, 1)))
            with eng.Fori(0, 3) as i:
                hg_stage(eng, what, 2 * i + 2, 0, slots(20 * n, put_out(eng, 2 * i, 0),
                                                        attend(eng, 2 * i + 1, 1),
                                                        take_in(eng, 2 * i + 2, 0)))
                hg_stage(eng, what, 2 * i + 3, 1, slots(20 * n, put_out(eng, 2 * i + 1, 1),
                                                        attend(eng, 2 * i + 2, 0),
                                                        take_in(eng, 2 * i + 3, 1)))

            def last_turn():
                yield from slots(20 * n, put_out(eng, 6, 0), attend(eng, 7, 1))
                yield from put_out(eng, 7, 1)

            if what == "pe":
                eng.wait_ge(hg_vec_out.sem, hg_vec_out.count("lo", 5))
            split_product(eng, what, "hgout", os_, last_turn(), m, 8, "n2")

        def gate_scalar(act):
            act.wait_ge(gate_in, 32)
            nc.scalar.activation(tls[:, 0], tl[:], ACT.Copy).then_inc(gt_act.sem, 1)
            nc.scalar.activation(ea[:], gaw[:, 0:8], ACT.Exp).then_inc(gt_act.sem, 1)
            yield from pause(7)
            act.wait_ge(gt_vec.sem, gt_vec.count("a"))
            lg = ps[:, 0, 0:32].rearrange("p (c n) -> p c n", c=2)
            for c in range(2):
                ins = nc.scalar.activation(gts[:, c, 0:8], lg[:, c, 0:8], ACT.Sigmoid, scale=rrc[:, c:c + 1])
            ins.then_inc(gt_act.sem, 1)
            nc.scalar.activation(gt2[:, 1], gt2[:, 0], ACT.Abs).then_inc(gt_act.sem, 1)
            act.wait_ge(gt_act.sem, gt_act.count("abs"))
            nc.scalar.activation(gt2[:, 1], gt2[:, 1], ACT.Exp, scale=-1.0).then_inc(gt_act.sem, 1)
            act.wait_ge(gt_act.sem, gt_act.count("e"))
            nc.scalar.activation(gt2[:, 1], gt2[:, 1], ACT.Ln, bias=1.0).then_inc(gt_act.sem, 1)
            yield from pause(3)
            act.wait_ge(gt_vec.sem, gt_vec.count("cum"))
            nc.scalar.activation(gt2[:, 2], gt2[:, 3], ACT.Exp).then_inc(gt_act.sem, 1)
            act.wait_ge(gt_vec.sem, gt_vec.count("tot"))
            nc.scalar.activation(gt2[:, 4], gt2[:, 4], ACT.Exp).then_inc(gt_act.sem, 1)

        def gate_vector(dve):
            dve.wait_ge(gt_act.sem, gt_act.count("tlh"))
            nc.vector.tensor_tensor(tls[:, 1], tl[:], tls[:, 0].bitcast(F32), ALU.subtract).then_inc(gt_vec.sem, 1)
            yield from pause(6)
            dve.wait_ge(gt_pe.sem, gt_pe.count("lg"))
            lg = ps[:, 0, 0:32].rearrange("p (c n) -> p c n", c=2)
            nc.vector.tensor_copy(rrc[:], ps[:, 0, 32:34]).then_inc(gt_vec.sem, 1)
            dve.wait_ge(gt_vec.sem, gt_vec.count("rr"))
            for c in range(2):
                ins = nc.vector.scalar_tensor_tensor(gt2[:, 0, c], lg[:, c, 8:16], rrc[:, c:c + 1],
                                                     gaw[:, 8:16], ALU.mult, ALU.add)
            ins.then_inc(gt_vec.sem, 1)
            yield from pause(2)
            dve.wait_ge(gt_act.sem, gt_act.count("l"))
            nc.vector.scalar_tensor_tensor(gt2[:, 2], gt2[:, 0], 0.0, gt2[:, 1], ALU.max,
                                                       ALU.add).then_inc(gt_vec.sem, 1)
            dve.wait_ge(gt_vec.sem, gt_vec.count("sp"))
            nc.vector.scalar_tensor_tensor(
                gts[:, :, 8:16], gt2[:, 2], -1.0, ea[:].unsqueeze(1).broadcast_to([P, 2, 8]),
                ALU.mult, ALU.mult).then_inc(gt_vec.sem, 1)
            yield
            dve.wait_ge(gt_pe.sem, gt_pe.count("cum"))
            nc.vector.tensor_copy(gt2[:, 3].rearrange("p c n -> p (c n)"), ps[:, 1, 0:16]).then_inc(gt_vec.sem, 1)
            dve.wait_ge(gt_vec.sem, gt_vec.count("cum"))
            nc.vector.tensor_tensor(gt2[:, 4].rearrange("p c n -> p (c n)"), ps[:, 1, 16:32],
                                                gt2[:, 3].rearrange("p c n -> p (c n)"), ALU.subtract).then_inc(gt_vec.sem, 1)
            yield from pause(2)
            dve.wait_ge(gt_act.sem, gt_act.count("egc"))
            nc.vector.tensor_tensor(gt2[:, 5], gt2[:, 2], gts[:, :, 0:8], ALU.mult).then_inc(gt_vec.sem, 1)

        def gate_tensor(pe):
            yield from pause(7)
            pe.wait_ge(gt_vec.sem, gt_vec.count("tll"))
            for c in range(2):
                yield from pause(2)
                o = ps[:, 0, 16 * c:16 * c + 16]
                for kt in range(DT):
                    hi = hs[:, kt, c * P:(c + 1) * P]
                    nc.tensor.matmul(o, hi, tls[:, 0, kt, :], start=(kt == 0), stop=False)
                    nc.tensor.matmul(o, hi, tls[:, 1, kt, :], start=False, stop=False)
                    mm = nc.tensor.matmul(o, hs[:, kt, T + c * P:T + (c + 1) * P], tls[:, 0, kt, :],
                                          start=False, stop=(kt == DT - 1))
            pe.wait_ge(norm_act.sem, norm_act.count("n5_r"))
            for c in range(2):
                mm = nc.tensor.matmul(ps[:, 0, 32 + c:33 + c], rr[:, c * P:(c + 1) * P], ident[:, 0:1],
                                      start=True, stop=True)
            mm.then_inc(gt_pe.sem, 1)
            yield from pause(6)
            pe.wait_ge(gt_vec.sem, gt_vec.count("g"))
            for c in range(2):
                nc.tensor.matmul(ps[:, 1, 8 * c:8 * c + 8], row_le, gts[:, c, 8:16], start=True, stop=True)
                mm = nc.tensor.matmul(ps[:, 1, 16 + 8 * c:24 + 8 * c], ones, gts[:, c, 8:16], start=True,
                                      stop=True)
            mm.then_inc(gt_pe.sem, 1)

        def mix_stage(eng, what, first, groups, dest, side):
            for k in range(4 * groups):
                grp, kb = divmod(k, 4)
                k_, g = 4 * first + k, GROUP_AT["mix"] + first + grp
                lap, par = BLOCK_AT["mix"] // SLOTS, g % 2
                if what == "act":
                    round_hi(eng, lap, k_ + AHEAD)
                    next(side, None)
                    if kb == 3:
                        copy_half(eng, lap, k_, g, par)
                elif what == "dve":
                    take_lo(eng, lap, k_ + AHEAD)
                    next(side, None)
                    if kb == 3:
                        evacuate_scaled(eng, dest(grp), g, par, 16, "n5")
                else:
                    multiply(eng, lap, k_, g, par, hs, kb, 0, 3, side,
                             "n5" if first == 0 and grp == 0 else None)
            drain(side)

        def sb_tensor(pe, t, par):
            pe.wait_ge(evac, GROUP_AT["mix"] + 3 * t + 2 + 3)
            if t == 0:
                pe.wait_ge(gt_vec.sem, gt_vec.count("tot"))
            else:
                pe.wait_ge(sb_vec.sem, sb_vec.count("lo", t - 1))
            q, k, v = (sin[:, par, s] for s in range(3))
            for h in range(2):
                nc.tensor.matmul(ps[:, h, 0:T], k[:, h * T:h * T + P], q[:, h * T:(h + 1) * T],
                                 start=True, stop=True)
                nc.tensor.matmul(ps[:, h, T:T + P], k[:, h * T + P:(h + 1) * T],
                                 q[:, h * T + P:(h + 1) * T], start=True, stop=True)
            for a in range(4):
                mm = nc.tensor.transpose(ps[:, 2, a * P:(a + 1) * P], v[:, a * P:(a + 1) * P], ident)
            mm.then_inc(sb_pe.sem, 1)
            yield from pause(7)
            pe.wait_ge(sb_vec.sem, sb_vec.count("sp", t))
            for h in range(2):
                nc.tensor.matmul(ps[:, h, 0:T], row_ge, sp_[:, h, 0:T], start=True, stop=False)
                nc.tensor.matmul(ps[:, h, P:T], ones, sp_[:, h, T:T + P], start=False, stop=True)
                mm = nc.tensor.matmul(ps[:, h, T:T + P], row_ge, sp_[:, h, T:T + P], start=True, stop=True)
            mm.then_inc(sb_pe.sem, 1)
            yield from pause(5)
            pe.wait_ge(sb_act.sem, sb_act.count("w", t))
            for h in range(2):
                nc.tensor.matmul(ps[:, 3, h * T:(h + 1) * T], svn[:, 2 * h, :], se[:, h, 0:T],
                                 start=True, stop=False)
                mm = nc.tensor.matmul(ps[:, 3, h * T + P:(h + 1) * T], svn[:, 2 * h + 1, :],
                                      se[:, h, T:T + P], start=False, stop=True)
            mm.then_inc(sb_pe.sem, 1)

        def sb_scalar(act, t, par):
            yield
            act.wait_ge(sb_pe.sem, sb_pe.count("z", t))
            nc.scalar.activation(svn[:].rearrange("p a b -> p (a b)"), ps[:, 2, :], ACT.Copy).then_inc(sb_act.sem, 1)
            act.wait_ge(sb_vec.sem, sb_vec.count("zm", t))
            nc.scalar.activation(se[:], zm[:], ACT.Abs).then_inc(sb_act.sem, 1)
            act.wait_ge(sb_act.sem, sb_act.count("abs", t))
            nc.scalar.activation(se[:], se[:], ACT.Exp, scale=-1.0).then_inc(sb_act.sem, 1)
            act.wait_ge(sb_act.sem, sb_act.count("e", t))
            nc.scalar.activation(se[:], se[:], ACT.Ln, bias=1.0).then_inc(sb_act.sem, 1)
            yield
            yield
            yield
            act.wait_ge(sb_vec.sem, sb_vec.count("w", t))
            nc.scalar.activation(se[:], zm[:], ACT.Exp).then_inc(sb_act.sem, 1)
            yield
            yield
            act.wait_ge(sb_pe.sem, sb_pe.count("o", t))
            nc.scalar.activation(mixs[:, 2 * t:2 * t + 2, 0:T],
                                             ps[:, 3, :].rearrange("p (h n) -> p h n", h=2), ACT.Copy).then_inc(sb_act.sem, 1)

        def sb_vector(dve, t, par):
            yield
            dve.wait_ge(sb_pe.sem, sb_pe.count("z", t))
            if t == 0:
                dve.wait_ge(neg_in, 16)
            nc.vector.scalar_tensor_tensor(
                zm[:], ps[:, 0:2, 0:384], float(P) ** -0.5, neg[:].unsqueeze(1).broadcast_to([P, 2, 384]),
                ALU.mult, ALU.add).then_inc(sb_vec.sem, 1)
            yield
            dve.wait_ge(sb_act.sem, sb_act.count("l", t))
            nc.vector.scalar_tensor_tensor(sp_[:], zm[:], 0.0, se[:], ALU.max, ALU.add).then_inc(sb_vec.sem, 1)
            yield
            yield
            dve.wait_ge(sb_pe.sem, sb_pe.count("cs", t))
            nc.vector.tensor_tensor(zm[:], zm[:], ps[:, 0:2, 0:384], ALU.subtract).then_inc(sb_vec.sem, 1)
            yield
            yield
            dve.wait_ge(sb_act.sem, sb_act.count("hi", t))
            nc.vector.tensor_tensor(
                mixs[:, 2 * t:2 * t + 2, T:2 * T], ps[:, 3, :].rearrange("p (h n) -> p h n", h=2),
                mixs[:, 2 * t:2 * t + 2, 0:T].bitcast(F32), ALU.subtract).then_inc(sb_vec.sem, 1)

        def col(a):
            return slice(a * P, (a + 1) * P)

        def gd_vector(dve, t, par):
            dve.wait_ge(evac, GROUP_AT["mix"] + 12 + 4 * t + 3 + 3)
            if t == 0:
                dve.wait_ge(gpad_set, 1)
            for j in range(4):
                for s in range(3):
                    for h in range(2):
                        c = VEC_AT["gdn_conv"] + (s * 8 + 2 * t + h) * 4 + j
                        y, src = gy[:, s, h * T:(h + 1) * T], gin[:, par, s, h, j:j + T]
                        if j == 0:
                            ins = nc.vector.tensor_scalar(y, src, vec[:, c:c + 1], None, ALU.mult)
                        else:
                            dve.wait_ge(gd_vec.sem, gd_vec.count(f"c{j - 1}", t))
                            ins = nc.vector.scalar_tensor_tensor(y, src, vec[:, c:c + 1], y, ALU.mult, ALU.add)
                ins.then_inc(gd_vec.sem, 1)
                if j == 1:
                    yield
            yield
            for h in range(2):
                for c in range(2):
                    ins = nc.vector.tensor_scalar(gbm[:, 2 * h + c, :], ones, gts[:, c, 8 + 2 * t + h:9 + 2 * t + h],
                                                  None, ALU.mult)
            ins.then_inc(gd_vec.sem, 1)
            for h in range(2):
                for c in range(2):
                    ins = nc.vector.tensor_scalar(bbm[:, 2 * h + c, :], ones, gts[:, c, 2 * t + h:1 + 2 * t + h],
                                                  -1.0, ALU.mult, ALU.mult)
            ins.then_inc(gd_vec.sem, 1)
            yield from pause(2)
            dve.wait_ge(gd_act.sem, gd_act.count("r", t))
            nc.vector.scalar_tensor_tensor(gy[:, 0], gy[:, 0], float(P) ** -0.5, gr[:, 0:2 * T],
                                                       ALU.mult, ALU.mult).then_inc(gd_vec.sem, 1)
            nc.vector.tensor_tensor(gy[:, 1], gy[:, 1], gr[:, 2 * T:4 * T], ALU.mult).then_inc(gd_vec.sem, 1)
            dve.wait_ge(gd_pe.sem, gd_pe.count("rows", t))
            for h in range(2):
                for c in range(2):
                    ins = nc.vector.tensor_scalar(DTr[:, 2 * h + c, :], ps[:, 2, col(2 * h + c)],
                                                  gt2[:, 3, c, 2 * t + h:2 * t + h + 1], 0.0,
                                                  ALU.subtract, ALU.min)
            ins.then_inc(gd_vec.sem, 1)
            yield
            yield
            flat = "p a b -> p (a b)"
            dve.wait_ge(gd_pe.sem, gd_pe.count("kk", t))
            dve.wait_ge(gd_act.sem, gd_act.count("dt", t))
            nc.vector.tensor_tensor(NLT[:].rearrange(flat), ps[:, 0, :], DTr[:].rearrange(flat),
                                                ALU.mult).then_inc(gd_vec.sem, 1)
            nc.vector.tensor_tensor(ATr[:].rearrange(flat), ps[:, 1, :], DTr[:].rearrange(flat),
                                                ALU.mult).then_inc(gd_vec.sem, 1)
            dve.wait_ge(gd_vec.sem, gd_vec.count("nl0", t))
            nc.vector.tensor_tensor(NLT[:].rearrange(flat), NLT[:].rearrange(flat), ps[:, 3, :],
                                                ALU.mult).then_inc(gd_vec.sem, 1)
            dve.wait_ge(gd_vec.sem, gd_vec.count("at0", t))
            nc.vector.tensor_tensor(ATr[:], ATr[:], row_le.unsqueeze(1).broadcast_to([P, 4, P]),
                                                ALU.mult).then_inc(gd_vec.sem, 1)
            q1 = gy[:, 0].rearrange("p (h c n) -> p h c n", h=2, c=2)[:, :, 1, :]
            nc.vector.tensor_tensor(qd[:], qd[:], q1, ALU.mult).then_inc(gd_vec.sem, 1)
            nc.vector.tensor_copy(Tm[:], ident.unsqueeze(1).broadcast_to([P, 4, P])).then_inc(gd_vec.sem, 1)
            nc.vector.memset(Y[:], 0.0)
            nc.vector.tensor_copy(TT[:], ident.unsqueeze(1).broadcast_to([P, 4, P])).then_inc(gd_vec.sem, 1)
            yield
            for lv in range(LEVELS):
                dve.wait_ge(gd_pe.sem, gd_pe.count(f"z{lv}", t))
                if lv == 0:
                    dve.wait_ge(gd_vec.sem, gd_vec.count("TT", t))
                else:
                    dve.wait_ge(gd_vec.sem, gd_vec.count(f"tt{lv - 1}", t))
                m_ = msk[:, LEVELS - 1 - lv, :]
                for u, (to, w) in enumerate(((Tm, "t"), (TT, "tt"))):
                    dve.sem_inc(copies_begun, 1)
                    nc.vector.copy_predicated(
                        half4(to[:].rearrange(flat), lv, u),
                        half_of(m_, LEVELS - 1 - lv, u).unsqueeze(1).broadcast_to(
                            [P, 4, 64 >> lv, 1 << lv]),
                        half4(ps[:, 1, :], lv, u)).then_inc(gd_vec.sem, 1)
                yield
            yield
            dve.wait_ge(gd_pe.sem, gd_pe.count("S", t))
            nc.vector.tensor_copy(Sm[:].rearrange(flat), ps[:, 2, 0:2 * P]).then_inc(gd_vec.sem, 1)

        def half4(ap, lv, u):
            return ap.rearrange("p (a n u h) -> p a n u h", a=4, u=2, h=1 << lv)[:, :, :, u, :]

        o_sq, o_rms, o_out = (b[:].rearrange("p a b -> p (a b)") for b in (NLT, Tm, Y))

        def gd_vector_out(dve, t, par):
            yield from pause(2)
            dve.wait_ge(gd_act_out.sem, gd_act_out.count("or", t))
            og, gain = o_out, vec[:, VEC_AT["gdn_gain"]:VEC_AT["gdn_gain"] + 1]
            nc.vector.scalar_tensor_tensor(og, ps[:, 0, :], gain, o_rms, ALU.mult,
                                                       ALU.mult).then_inc(gd_vec_out.sem, 1)
            dve.wait_ge(gd_vec_out.sem, gd_vec_out.count("og", t))
            o2 = og.rearrange("p (h n) -> p h n", h=2)
            nc.vector.tensor_tensor(o2, o2, gin[:, par, 3, :, 3:3 + T], ALU.mult).then_inc(gd_vec_out.sem, 1)
            dve.wait_ge(gd_vec_out.sem, gd_vec_out.count("os", t))
            dst = mixs[:, 8 + 2 * t:10 + 2 * t, :]
            nc.vector.tensor_scalar(dst[:, :, 0:T], o2, 1.0, None, ALU.mult).then_inc(gd_vec_out.sem, 1)
            dve.wait_ge(gd_vec_out.sem, gd_vec_out.count("hi", t))
            nc.vector.tensor_tensor(dst[:, :, T:2 * T], o2, dst[:, :, 0:T].bitcast(F32),
                                                ALU.subtract).then_inc(gd_vec_out.sem, 1)

        def gd_scalar(act, t, par):
            flat = "p a b -> p (a b)"
            yield
            yield
            act.wait_ge(gd_vec.sem, gd_vec.count("c3", t))
            nc.scalar.activation(gin[:, par, 3, :, 3:3 + T], gin[:, par, 3, :, 3:3 + T], ACT.Silu)
            nc.scalar.activation(gy[:], gy[:], ACT.Silu).then_inc(gd_act.sem, 1)
            act.wait_ge(gd_act.sem, gd_act.count("silu", t))
            nc.scalar.activation(gs[:], gy[:, 0:2, :].rearrange("p a b -> p (a b)"), ACT.Square).then_inc(gd_act.sem, 1)
            yield
            yield
            act.wait_ge(gd_pe.sem, gd_pe.count("ssq", t))
            nc.scalar.activation(gr[:].rearrange("p (a b) -> p a b", a=2), ps[:, 0:2, :], ACT.Ln,
                                             bias=EPS).then_inc(gd_act.sem, 1)
            act.wait_ge(gd_act.sem, gd_act.count("ln", t))
            nc.scalar.activation(gr[:], gr[:], ACT.Exp, scale=-0.5).then_inc(gd_act.sem, 1)
            rows = ps[:, 2, :].rearrange("p (h c n) -> p h c n", h=2, c=2)
            act.wait_ge(gd_vec.sem, gd_vec.count("d", t))
            nc.scalar.activation(qd[:], rows[:, :, 1, :], ACT.Exp).then_inc(gd_act.sem, 1)
            nc.scalar.activation(DTr[:], DTr[:], ACT.Exp).then_inc(gd_act.sem, 1)
            yield
            yield
            yield
            act.wait_ge(gd_pe.sem, gd_pe.count("tr", t))
            for h in range(2):
                for c in range(2):
                    ins = nc.scalar.activation(vb[:, 2 * h + c, :], ps[:, 3, col(2 * h + c)], ACT.Copy,
                                               scale=gts[:, c, 2 * t + h:2 * t + h + 1])
            ins.then_inc(gd_act.sem, 1)
            for h in range(2):
                ins = nc.scalar.activation(kbe[:, h, :], ps[:, 2, col(2 * h + 1)], ACT.Copy,
                                           scale=gt2[:, 5, 1, 2 * t + h:2 * t + h + 1])
            ins.then_inc(gd_act.sem, 1)
            for h in range(2):
                ins = nc.scalar.activation(ktl[:, h, :], ps[:, 2, col(2 * h)], ACT.Copy,
                                           scale=gt2[:, 4, 0, 2 * t + h:2 * t + h + 1])
            ins.then_inc(gd_act.sem, 1)
            for lv in range(LEVELS):
                act.wait_ge(gd_pe.sem, gd_pe.count(f"y{lv}", t))
                nc.scalar.activation(half4(Y[:].rearrange(flat), lv, 0), half4(ps[:, 0, :], lv, 0),
                                                 ACT.Copy).then_inc(gd_act.sem, 1)
                yield
            act.wait_ge(gd_pe.sem, gd_pe.count("uw", t))
            nc.scalar.activation(u0[:].rearrange(flat), ps[:, 0, 0:2 * P], ACT.Copy).then_inc(gd_act.sem, 1)
            nc.scalar.activation(nwT[:].rearrange(flat), ps[:, 1, 0:2 * P], ACT.Copy,
                                             scale=-1.0).then_inc(gd_act.sem, 1)

        def gd_scalar_out(act, t, par):
            flat = "p a b -> p (a b)"
            act.wait_ge(gd_pe_out.sem, gd_pe_out.count("vn", t))
            nc.scalar.activation(vnw[:].rearrange(flat), ps[:, 3, 0:2 * P], ACT.Copy).then_inc(gd_act_out.sem, 1)
            yield
            act.wait_ge(gd_pe_out.sem, gd_pe_out.count("o", t))
            nc.scalar.activation(o_sq, ps[:, 0, :], ACT.Square).then_inc(gd_act_out.sem, 1)
            yield
            act.wait_ge(gd_pe_out.sem, gd_pe_out.count("os", t))
            nc.scalar.activation(o_rms, ps[:, 1, :], ACT.Ln, bias=EPS, scale=1.0 / P).then_inc(gd_act_out.sem, 1)
            act.wait_ge(gd_act_out.sem, gd_act_out.count("oln", t))
            nc.scalar.activation(o_rms, o_rms, ACT.Exp, scale=-0.5).then_inc(gd_act_out.sem, 1)

        def gd_tensor(pe, t, par):
            yield from pause(7)
            pe.wait_ge(gd_act.sem, gd_act.count("sqk", t))
            if t == 0:
                pe.wait_ge(sb_vec.sem, sb_vec.count("lo", 3))
            else:
                pe.wait_ge(gd_vec_out.sem, gd_vec_out.count("og", t - 1))
            for b in range(2):
                mm = nc.tensor.matmul(ps[:, b, :], ones, gs[:, b * 2 * T:(b + 1) * 2 * T], start=True, stop=True)
            mm.then_inc(gd_pe.sem, 1)
            pe.wait_ge(gd_vec.sem, gd_vec.count("bbm", t))
            for a in range(4):
                nc.tensor.matmul(ps[:, 2, col(a)], gbm[:, a, :], row_le, start=True, stop=True)
                mm = nc.tensor.matmul(ps[:, 3, col(a)], bbm[:, a, :], ident, start=True, stop=True)
            mm.then_inc(gd_pe.sem, 1)
            yield from pause(4)
            pe.wait_ge(gd_vec.sem, gd_vec.count("k", t))
            for a in range(4):
                nc.tensor.matmul(ps[:, 0, col(a)], gy[:, 1, col(a)], gy[:, 1, col(a)], start=True, stop=True)
                mm = nc.tensor.matmul(ps[:, 1, col(a)], gy[:, 1, col(a)], gy[:, 0, col(a)], start=True, stop=True)
            mm.then_inc(gd_pe.sem, 1)
            yield from pause(2)
            pe.wait_ge(gd_vec.sem, gd_vec.count("TT", t))
            pe.wait_ge(gd_act.sem, gd_act.count("qe", t))
            for a in range(4):
                nc.tensor.transpose(ps[:, 2, col(a)], gy[:, 1, col(a)], ident)
                mm = nc.tensor.transpose(ps[:, 3, col(a)], gy[:, 2, col(a)], ident)
            mm.then_inc(gd_pe.sem, 1)
            yield
            for lv in range(LEVELS):
                if lv:
                    pe.wait_ge(gd_vec.sem, gd_vec.count(f"tt{lv - 1}", t))
                for a in range(4):
                    mm = nc.tensor.matmul(half_of(ps[:, 0, col(a)], LEVELS - 1 - lv, 0), NLT[:, a, :],
                                          half_of(Tm[:, a, :], LEVELS - 1 - lv, 0), start=True, stop=True)
                mm.then_inc(gd_pe.sem, 1)
                yield
                pe.wait_ge(gd_act.sem, gd_act.count(f"y{lv}", t))
                for a in range(4):
                    y, tt = Y[:, a, :], TT[:, a, :]
                    nc.tensor.matmul(half_of(ps[:, 1, col(a)], LEVELS - 1 - lv, 0), tt,
                                     half_of(y, LEVELS - 1 - lv, 0), start=True, stop=True)
                    mm = nc.tensor.matmul(half_of(ps[:, 1, col(a)], LEVELS - 1 - lv, 1), y,
                                          half_of(tt, LEVELS - 1 - lv, 1), start=True, stop=True)
                mm.then_inc(gd_pe.sem, 1)
                yield
            pe.wait_ge(gd_vec.sem, gd_vec.count(f"tt{LEVELS - 1}", t))
            pe.wait_ge(gd_act.sem, gd_act.count("ktl", t))
            for h in range(2):
                nc.tensor.matmul(ps[:, 0, col(h)], TT[:, 2 * h, :], vb[:, 2 * h, :], start=True, stop=True)
                mm = nc.tensor.matmul(ps[:, 1, col(h)], kbe[:, h, :], TT[:, 2 * h + 1, :], start=True, stop=True)
            mm.then_inc(gd_pe.sem, 1)
            yield
            pe.wait_ge(gd_act.sem, gd_act.count("nw", t))
            for h in range(2):
                mm = nc.tensor.matmul(ps[:, 2, col(h)], ktl[:, h, :], u0[:, h, :], start=True, stop=True)
            mm.then_inc(gd_pe.sem, 1)

        def gd_tensor_out(pe, t, par):
            pe.wait_ge(gd_vec.sem, gd_vec.count("S", t))
            for h in range(2):
                nc.tensor.matmul(ps[:, 3, col(h)], TT[:, 2 * h + 1, :], vb[:, 2 * h + 1, :], start=True, stop=False)
                mm = nc.tensor.matmul(ps[:, 3, col(h)], nwT[:, h, :], Sm[:, h, :], start=False, stop=True)
            mm.then_inc(gd_pe_out.sem, 1)
            yield
            pe.wait_ge(gd_act_out.sem, gd_act_out.count("vn", t))
            for h in range(2):
                nc.tensor.matmul(ps[:, 0, col(2 * h)], u0[:, h, :], ATr[:, 2 * h, :], start=True, stop=True)
                nc.tensor.matmul(ps[:, 0, col(2 * h + 1)], vnw[:, h, :], ATr[:, 2 * h + 1, :], start=True, stop=False)
                mm = nc.tensor.matmul(ps[:, 0, col(2 * h + 1)], Sm[:, h, :], qd[:, h, :], start=False, stop=True)
            mm.then_inc(gd_pe_out.sem, 1)
            yield from pause(2)
            pe.wait_ge(gd_act_out.sem, gd_act_out.count("osq", t))
            nc.tensor.matmul(ps[:, 1, :], ones, o_sq, start=True, stop=True).then_inc(gd_pe_out.sem, 1)

        def mix_all(eng, what, gates_, attend, delta, put_out):
            n = 2 if what == "pe" else 1

            def qkv(par):
                return lambda s: sin[:, par, s].rearrange("p (h n) -> p h n", h=2)

            def qkvz(par):
                return lambda s: gin[:, par, s, :, 3:3 + T]

            for t in range(4):
                mix_stage(eng, what, 3 * t, 3, qkv(t % 2), attend(eng, t - 1, (t - 1) % 2) if t else gates_)
            for t in range(4):
                if t == 0:
                    side = attend(eng, 3, 1)
                elif t == 1:
                    side = slots(16 * n, delta(eng, 0, 0))
                else:
                    side = slots(16 * n, put_out(eng, t - 2, t % 2), delta(eng, t - 1, (t - 1) % 2))
                mix_stage(eng, what, 12 + 4 * t, 4, qkvz(t % 2), side)

            def last_turn():
                yield from slots(16 * n, put_out(eng, 2, 0), delta(eng, 3, 1))
                yield from put_out(eng, 3, 1)

            if what == "pe":
                eng.wait_ge(gd_vec_out.sem, gd_vec_out.count("lo", 1))
            split_product(eng, what, "mixout", mixs, last_turn(), x, 16, "n8", "xattn")

        def cross_tensor(pe):
            pe.wait_ge(evac, GROUP_AT["kv"] + 3 + 3)
            for h in range(4):
                for c in range(2):
                    mm = nc.tensor.matmul(ps[:, h, c * T:(c + 1) * T], xq[:, h, col(c)], kv[:, h, :],
                                          start=True, stop=True)
            mm.then_inc(xa_pe.sem, 1)
            pe.wait_ge(xa_act.sem, xa_act.count("p"))
            for h in range(4):
                for c in range(2):
                    mm = nc.tensor.transpose(ps[:, h // 2, (h % 2 * 2 + c) * P:(h % 2 * 2 + c + 1) * P],
                                             kv[:, 4 + h, col(c)], ident)
            mm.then_inc(xa_pe.sem, 1)
            pe.wait_ge(xa_act.sem, xa_act.count("vn"))
            pe.wait_ge(xa_vec.sem, xa_vec.count("p"))
            for h in range(4):
                for c in range(2):
                    for b in range(2):
                        mm = nc.tensor.transpose(ps[:, h, c * T + b * P:c * T + (b + 1) * P],
                                                 pr[:, 2 * h + b, col(c)], ident)
            mm.then_inc(xa_pe.sem, 1)
            pe.wait_ge(xa_act.sem, xa_act.count("pt"))
            for h in range(4):
                for c in range(2):
                    mm = nc.tensor.matmul(ps[:, h // 2, h % 2 * T:(h % 2 + 1) * T], xvn[:, h, c, :],
                                          prT[:, h, c, :], start=(c == 0), stop=(c == 1))
            mm.then_inc(xa_pe.sem, 1)

        def cross_scalar(act):
            act.wait_ge(xa_vec.sem, xa_vec.count("nmx"))
            for a in range(8):
                ins = nc.scalar.activation(pr[:, a, :], ps[:, a // 2, a % 2 * T:(a % 2 + 1) * T], ACT.Exp,
                                           bias=mx[:, a:a + 1], scale=float(P) ** -0.5, accum_out=sm[:, a:a + 1])
            ins.then_inc(xa_act.sem, 1)
            act.wait_ge(xa_pe.sem, xa_pe.count("vt"))
            nc.scalar.activation(xvn[:].rearrange("p h c n -> p (h c n)").rearrange(
                "p (a b) -> p a b", a=2), ps[:, 0:2, :], ACT.Copy).then_inc(xa_act.sem, 1)
            act.wait_ge(xa_pe.sem, xa_pe.count("pt"))
            nc.scalar.activation(prT[:].rearrange("p h c n -> p h (c n)"), ps[:], ACT.Copy).then_inc(xa_act.sem, 1)
            act.wait_ge(xa_pe.sem, xa_pe.count("o"))
            nc.scalar.activation(xs[:, :, 0:T], ps[:, 0:2, :].rearrange(
                "p a (b n) -> p (a b) n", b=2), ACT.Copy).then_inc(xa_act.sem, 1)

        def cross_vector(dve):
            dve.wait_ge(xa_pe.sem, xa_pe.count("z"))
            nc.vector.reduce_max(mx[:], ps[:].rearrange("p h (c n) -> p (h c) n", c=2), AXX).then_inc(xa_vec.sem, 1)
            dve.wait_ge(xa_vec.sem, xa_vec.count("mx"))
            nc.vector.tensor_scalar(mx[:], mx[:], -float(P) ** -0.5, None, ALU.mult).then_inc(xa_vec.sem, 1)
            dve.wait_ge(xa_act.sem, xa_act.count("p"))
            nc.vector.reciprocal(rs[:], sm[:]).then_inc(xa_vec.sem, 1)
            dve.wait_ge(xa_vec.sem, xa_vec.count("rs"))
            nc.vector.tensor_tensor(pr[:], pr[:], rs[:].unsqueeze(2).broadcast_to([P, 8, T]),
                                                ALU.mult).then_inc(xa_vec.sem, 1)
            dve.wait_ge(xa_act.sem, xa_act.count("hi"))
            nc.vector.tensor_tensor(xs[:, :, T:2 * T], ps[:, 0:2, :].rearrange(
                "p a (b n) -> p (a b) n", b=2), xs[:, :, 0:T].bitcast(F32), ALU.subtract).then_inc(xa_vec.sem, 1)

        def mlp(eng, what, which):
            name, cname = ("up1", "conv1") if which == 0 else ("up2", "conv2")
            first = 1 + which
            va, aa = mlp_vec[which], mlp_act[which]
            lap0, g0 = BLOCK_AT[name] // SLOTS, GROUP_AT[name]
            if what == "dve":
                nc.vector.memset(cin[:, :, 0:first], 0.0).then_inc(pad_set[which], 1)
                if which == 0:
                    nc.vector.memset(cin[:, :, T + 1:T + 2], 0.0).then_inc(pad_set[which], 1)
            with eng.Fori(0, UP_GROUPS // 2) as i:
                lap, g = lap0 + 2 * i, g0 + 2 * i
                for k in range(8):
                    part, kb = divmod(k, 4)
                    if what == "act":
                        round_hi(eng, lap, k + AHEAD)
                        if kb == 3:
                            copy_half(eng, lap, k, g + part, part)
                            if part == 0:
                                eng.wait_ge(va.sem, va.count("a21", i))
                                nc.scalar.activation(cy[:, 0:2, :], cy[:, 0:2, :], ACT.Silu).then_inc(aa.sem, 1)
                    elif what == "dve":
                        take_lo(eng, lap, k + AHEAD)
                        if kb == 3:
                            evacuate_scaled(eng, cin[:, 2 * part:2 * part + 2, first:first + T], g + part,
                                            part, (8, 20)[which], ("n3", "n10")[which])
                            eng.wait_ge(evac, g + part + 3)
                            w = "ab"[part]
                            if part == 0:
                                eng.wait_ge(pad_set[which], 2 - which)
                            for tap in range(3):
                                for t in range(2):
                                    y, src = cy[:, 2 * part + t, :], cin[:, 2 * part + t, tap:tap + T]
                                    col = VEC_AT[cname] + (FT * part + 2 * i + t) * 4
                                    if tap == 0:
                                        ins = nc.vector.tensor_scalar(
                                            y, src, vec[:, bass.ds(col, 1)], vec[:, bass.ds(col + 3, 1)],
                                            ALU.mult, ALU.add)
                                    else:
                                        eng.wait_ge(va.sem, va.count(f"{w}{tap - 1}{t}", i))
                                        ins = nc.vector.scalar_tensor_tensor(
                                            y, src, vec[:, bass.ds(col + tap, 1)], y, ALU.mult, ALU.add)
                                    ins.then_inc(va.sem, 1)
                    else:
                        multiply(eng, lap, k, g + part, part, hs, kb, 0, 3,
                                 norm=("n3", "n10")[which] if part == 0 else None)
                if what == "dve":
                    eng.wait_ge(aa.sem, aa.count("silu", i))
                    eng.wait_ge(va.sem, va.count("b21", i))
                    nc.vector.tensor_tensor(cy[:, 0:2, :], cy[:, 0:2, :], cy[:, 2:4, :], ALU.mult).then_inc(va.sem, 1)
                    eng.wait_ge(va.sem, va.count("mul", i))
                    dst = acts[:, bass.ds(2 * i, 2), :]
                    nc.vector.tensor_scalar(dst[:, :, 0:T], cy[:, 0:2, :], 1.0, None, ALU.mult).then_inc(va.sem, 1)
                    eng.wait_ge(va.sem, va.count("hi", i))
                    nc.vector.tensor_tensor(dst[:, :, T:2 * T], cy[:, 0:2, :],
                                                    dst[:, :, 0:T].bitcast(F32), ALU.subtract).then_inc(va.sem, 1)

        def x_ready(s):
            return lambda eng, c: eng.wait_ge(norm_vec.sem, norm_vec.count(f"{s}_x{c}"))

        block = ctx.enter_context(nc.Block())

        @block.sync
        def _(sp):
            sp.dma_start(x[:], xT).then_inc(const_in, 16)
            sp.dma_start(vec[:], vecs).then_inc(const_in, 16)
            sp.dma_start(cst[:], consts[:, 0:4 * P].rearrange("p (a b) -> p a b", a=4)).then_inc(const_in, 16)
            sp.dma_start(G[:].rearrange("p a b -> p (a b)")[:, 0:LEVELS * P], masks).then_inc(const_in, 16)
            sp.dma_start(reset[:], consts[:, 4 * P:4 * P + 2 * T]).then_inc(const_in, 16)
            with sp.Fori(0, N_BLOCKS // SLOTS) as i:
                for b in range(SLOTS):
                    sp.wait_ge(lo_ready, SLOTS * i + b + 1)
                    sp.dma_start(raw[:, b, :], stream[SLOTS * i + b]).then_inc(raw_in[b], 16)

        @block.scalar
        def _(act):
            for s in (norm_act, hg_act_in, hg_act, hg_act_out, *mlp_act, gt_act, sb_act, gd_act, gd_act_out, xa_act):
                act.sem_inc(s.sem, 1)
            act.wait_ge(const_in, 80)
            for k in range(AHEAD):
                round_hi(act, 0, k)
            pre_scalar(act, "n1", "pre_mix", lambda e, c: None)
            act.wait_ge(hg_set, 2)
            lb2 = lb[:].rearrange("p a b -> p (a b)")
            nc.scalar.activation(lb2, lb2, ACT.Exp).then_inc(hg_exp, 1)
            hg_all(act, "act", hg_scalar_in, hg_scalar, hg_scalar_out)
            pre_scalar(act, "n3", "pre_ffn", x_ready("n2"))
            mlp(act, "act", 0)
            product(act, "act", "down1", DOWN_BLOCKS, 2, 4, then="n4")
            pre_scalar(act, "n5", "mix", x_ready("n4"))
            mix_all(act, "act", gate_scalar(act), sb_scalar, gd_scalar, gd_scalar_out)
            product(act, "act", "xq", 4, 1, 2, dest=xq, side=memory_scalar(act))
            product(act, "act", "kv", 4, 2, 2, dest=kv)
            cross_scalar(act)
            product(act, "act", "xo", 1, 2, 4, dest=x, then="n10", gain="ffn2")
            mlp(act, "act", 1)
            product(act, "act", "down2", DOWN_BLOCKS, 2, 4, last=True, dest=x, then="n12")

        @block.vector
        def _(dve):
            for s in (norm_vec, hg_vec_in, hg_vec, hg_vec_out, *mlp_vec, gt_vec, sb_vec, gd_vec, gd_vec_out, xa_vec):
                dve.sem_inc(s.sem, 1)
            dve.sem_inc(lo_ready, SLOTS)
            dve.sem_inc(evac, 2)
            dve.wait_ge(const_in, 80)
            for k in range(AHEAD):
                take_lo(dve, 0, k)
            pre_vector(dve, "n1", "pre_mix")
            bnd = vec[:, VEC_AT["bounds"]:VEC_AT["bounds"] + 2 * HEADS]
            lb2, oml2 = lb[:].rearrange("p a b -> p (a b)"), oml[:].rearrange("p a b -> p (a b)")
            nc.vector.tensor_copy(msk[:].rearrange("p l n -> p (l n)"),
                                  G[:].rearrange("p a b -> p (a b)")[:, 0:LEVELS * P])
            nc.vector.memset(lf[:, 0:1], 0.0).then_inc(hg_set, 1)
            nc.vector.tensor_tensor(lb2, bnd, bnd, ALU.subtract).then_inc(hg_set, 1)
            dve.wait_ge(hg_exp, 1)
            nc.vector.reciprocal(oml2, lb2).then_inc(hg_set, 1)
            dve.wait_ge(hg_set, 3)
            nc.vector.tensor_tensor(lb2, lb2, oml2, ALU.mult).then_inc(hg_set, 1)
            dve.wait_ge(hg_set, 4)
            nc.vector.tensor_tensor(lb2, lb2, lb2, ALU.subtract).then_inc(hg_set, 1)
            dve.wait_ge(hg_set, 5)
            nc.vector.tensor_scalar(oml2, lb2, -1.0, 1.0, ALU.mult, ALU.add).then_inc(hg_set, 1)
            dve.wait_ge(hg_set, 6)
            hg_all(dve, "dve", hg_vector_in, hg_vector, hg_vector_out)
            norm_post_vector(dve, "n2", "post_mix")
            pre_vector(dve, "n3", "pre_ffn")
            mlp(dve, "dve", 0)
            product(dve, "dve", "down1", DOWN_BLOCKS, 2, 4, then="n4")
            norm_post_vector(dve, "n4", "post_ffn")
            pre_vector(dve, "n5", "mix")
            nc.vector.memset(gin[:, :, :, :, 0:3], 0.0).then_inc(gpad_set, 1)
            mix_all(dve, "dve", gate_vector(dve), sb_vector, gd_vector, gd_vector_out)
            product(dve, "dve", "xq", 4, 1, 2, dest=xq, side=memory_vector(dve), plain=16)
            product(dve, "dve", "kv", 4, 2, 2, dest=kv)
            cross_vector(dve)
            product(dve, "dve", "xo", 1, 2, 4, dest=x, onto=True, plain=20, then="n10", gain="ffn2")
            mlp(dve, "dve", 1)
            product(dve, "dve", "down2", DOWN_BLOCKS, 2, 4, last=True, dest=x, onto=True, plain=20,
                    then="n12")
            final_vector(dve, "n12", "final")

        @block.tensor
        def _(pe):
            for s in (norm_pe, hg_pe, hg_pe_out, gt_pe, sb_pe, gd_pe, gd_pe_out, xa_pe):
                pe.sem_inc(s.sem, 1)
            pe.sem_inc(blk_used, SLOTS)
            pe.wait_ge(const_in, 80)
            pre_tensor(pe, "n1")
            hg_all(pe, "pe", lambda *a: pause(0), hg_tensor, hg_tensor_out)
            pre_tensor(pe, "n3")
            mlp(pe, "pe", 0)
            product(pe, "pe", "down1", DOWN_BLOCKS, 2, 4, acts, norm="up1", then="n4")
            pre_tensor(pe, "n5")
            mix_all(pe, "pe", gate_tensor(pe), sb_tensor, gd_tensor, gd_tensor_out)
            product(pe, "pe", "xq", 4, 1, 2, hs, side=memory_tensor(pe), norm="n8")
            product(pe, "pe", "kv", 4, 2, 2, mems, dest=kv, norm="n7")
            cross_tensor(pe)
            pe.wait_ge(xa_vec.sem, xa_vec.count("lo"))
            product(pe, "pe", "xo", 1, 2, 4, xs, then="n10")
            mlp(pe, "pe", 1)
            product(pe, "pe", "down2", DOWN_BLOCKS, 2, 4, acts, last=True, norm="up2", then="n12")

        @block.gpsimd
        def _(pool):
            pool.wait_ge(evac, GROUP_AT["down1"] + 7 + 3)
            pool.dma_start(tl[:], tail).then_inc(gate_in, 16)
            pool.dma_start(gaw[:], gates).then_inc(gate_in, 16)
            pool.dma_start(neg[:], consts[:, 4 * P + 2 * T:4 * P + 2 * T + 384]).then_inc(neg_in, 16)
            pool.wait_ge(gd_vec_out.sem, gd_vec_out.count("lo", 3))
            pool.wait_ge(gd_act_out.sem, gd_act_out.count("or", 3))
            pool.wait_ge(gd_pe_out.sem, gd_pe_out.count("os", 3))
            pool.dma_start(memr[:], memT).then_inc(mem_in, 16)
            pool.wait_ge(norm_vec.sem, norm_vec.count("n12_h3"))
            pool.dma_start(outT, sq[:]).then_inc(out_done, 16)
            pool.wait_ge(out_done, 16)


def tiles(a):
    return a.reshape(a.shape[0] // P, P, *a.shape[1:]).swapaxes(0, 1)


def blocks(w, order=None):
    k, n = w.shape
    a = w.reshape(k // 512, 4, P, n // 256, 256).transpose(3, 0, 2, 1, 4)
    if order is not None:
        a = a[np.array(order)]
    return a.reshape(-1, P, BLK)


def last_rows_last(b):
    b = b.reshape(8, 4, P, BLK)
    return np.concatenate([b[:, :3].reshape(24, P, BLK), b[:, 3]])


def lay_out(i):
    f32 = np.float32
    per_turn = [s * 8 + t for t in range(8) for s in (1, 2, 0, 4, 3)]
    per_pair = [s * (F // 256) + t for t in range(F // 256) for s in range(2)]
    mix = [s * 4 + t for t in range(4) for s in (0, 1, 2)]
    mix += [s * 4 + t for t in range(4) for s in (3, 4, 5, 6)]
    w_in2 = i["w_in_2"][0]
    stream = np.concatenate([
        blocks(i["hgrn_w_in"][0], per_turn), last_rows_last(blocks(i["hgrn_w_out"][0])),
        blocks(i["ffn_w_in"][0], per_pair), blocks(i["ffn_w_out"][0]),
        blocks(w_in2[:, :28 * 256], mix), last_rows_last(blocks(i["w_out_2"][0])), blocks(i["w_xq_2"][0]),
        blocks(i["w_xkv_2"][0]), blocks(i["w_xo_2"][0]), blocks(i["w_up_2"][0], per_pair),
        blocks(i["w_down_2"][0])])
    assert len(stream) == N_BLOCKS
    cols = lambda v: v.reshape(-1, P).T
    taps = lambda rows: tiles(np.stack(rows, 1)).reshape(P, -1)
    zero = np.zeros(2 * F, f32)
    parts = {
        "pre_mix": cols(i["norm_pre_mix"]), "post_mix": cols(i["norm_post_mix"]),
        "pre_ffn": cols(i["norm_pre_ffn"]), "post_ffn": cols(i["norm_post_ffn"]),
        "mix": cols(i["mix_norm_2"]), "xattn": cols(i["xattn_norm_2"]), "mem": cols(i["mem_norm_2"]),
        "ffn2": cols(i["ffn_norm_2"]), "final": cols(i["final_norm_2"]),
        "hgrn_gain": cols(i["hgrn_gnorm"]), "gdn_gain": cols(i["gdn_norm_2"]),
        "bounds": cols(i["hgrn_lower_bounds"]), "gdn_conv": taps(list(i["gdn_conv_2"][0])),
        "conv1": taps([*i["ffn_w_conv"][0], zero]),
        "conv2": taps([*i["ffn_conv_2"][0], i["ffn_conv_bias_2"][0]]),
    }
    vecs = np.concatenate([parts[n].astype(f32, copy=False) for n, _ in VEC_PARTS], 1)
    assert vecs.shape[1] == VEC_N
    at = np.arange(P)
    reset = np.ones((P, 2 * T), f32)
    reset[:, ::64] = 0
    ge = (at[:, None] >= at[None, :]).astype(f32)
    neg = np.zeros((P, 384), f32)
    neg[:, 0:P] = neg[:, 2 * P:] = -1e30 * ge
    consts = np.concatenate([np.eye(P, dtype=f32), np.ones((P, P), f32), ge, ge.T, reset, neg], 1)
    masks = np.zeros((P, LEVELS, P), f32)
    for lv in range(LEVELS):
        h = 64 >> lv
        low = (at // h % 2 == 0)
        same = at[:, None] // (2 * h) == at[None, :] // (2 * h)
        masks[:, lv] = same & (low[:, None] != low[None, :])
    gates = np.broadcast_to(np.concatenate([i["gdn_a_log_2"][0], i["gdn_dt_bias_2"][0]]), (P, 16))
    return {
        "xT": tiles(i["x"][0].T), "memT": tiles(i["mem_2"][0].T), "stream": stream,
        "tail": tiles(w_in2[:, 28 * 256:]), "vecs": vecs, "gates": gates, "consts": consts,
        "masks": masks.reshape(P, -1),
    }


def kernel(**inputs):
    import concourse.bacc as bacc
    from concourse.bass_utils import run_bass_kernel_spmd

    arrays = {n: np.ascontiguousarray(a) for n, a in lay_out(
        {n: np.asarray(a) for n, a in inputs.items()}).items()}
    nc = bacc.Bacc("TRN2", target_bir_lowering=False, num_devices=1)
    args = {n: nc.dram_tensor(n, a.shape, mybir.dt.from_np(a.dtype), kind="ExternalInput").ap()
            for n, a in arrays.items()}
    out = nc.dram_tensor("outT", (P, DT, T), F32, kind="ExternalOutput").ap()
    build(nc, **args, outT=out)
    got = run_bass_kernel_spmd(nc, [arrays], core_ids=[0]).results[0]["outT"]
    return np.ascontiguousarray(got.transpose(1, 0, 2).reshape(1, D, T).transpose(0, 2, 1))
```
